# Optimizing a Trainium2 kernel written in Bass

```python
import jax, jax.numpy as jnp
from jax import lax
import numpy as np

D_MODEL = 1024
BATCH = 1
SEQ = 128
DEPTH = 2
DEC_BATCH = 1
DEC_SEQ = 256
PAST_LEN = 128

GRID_W = 64
N_MIXERS = 2
N_HEADS = 16
N_KV_HEADS = 4
HEAD_DIM = D_MODEL // N_HEADS
Q_PER_KV = N_HEADS // N_KV_HEADS
ROPE_THETA = 10000.0
Q_BLOCK = 128
POOL_WINDOWS = (2, 4, 8, 16)
N_POOL_GROUPS = len(POOL_WINDOWS)
POOL_GROUP_DIM = D_MODEL // N_POOL_GROUPS
N_EXPERT_GROUPS = 4
EXPERTS_PER_GROUP = 8
N_EXPERTS = N_EXPERT_GROUPS * EXPERTS_PER_GROUP
TOP_K_IN_GROUP = 2
D_EXPERT = D_MODEL // 4
N_ATTN_LAYERS = (DEPTH + N_MIXERS - 1) // N_MIXERS
N_POOL_LAYERS = DEPTH // N_MIXERS
N_MOD = 6
EPS = 1e-6

kernel_name = "hybrid_diffusion_gqa_pool_hmoe_step"

F32 = jnp.float32

def rms_norm(x, g):
    xf = x.astype(F32)
    y = xf * lax.rsqrt(jnp.mean(xf * xf, axis=-1, keepdims=True) + EPS)
    return (y * g.astype(F32)).astype(x.dtype)

def ada_modulation(cond, w, b):
    m = jax.nn.silu(cond) @ w + b
    m = m.reshape(cond.shape[0], 1, N_MOD, D_MODEL)
    return tuple(m[:, :, i] for i in range(N_MOD))

def modulate(x, g, shift, scale):
    return rms_norm(x, g) * (1.0 + scale) + shift

def grid_rope_tables(length):
    rows = length // GRID_W
    row = jnp.broadcast_to(jnp.arange(rows, dtype=F32)[:, None], (rows, GRID_W)).reshape(-1)
    col = jnp.broadcast_to(jnp.arange(GRID_W, dtype=F32)[None, :], (rows, GRID_W)).reshape(-1)
    axis_dim = HEAD_DIM // 2
    inv_freq = jnp.power(ROPE_THETA, -jnp.arange(0, axis_dim, 2, dtype=F32) / axis_dim)
    ang = jnp.concatenate([row[:, None] * inv_freq, col[:, None] * inv_freq], axis=-1)
    return jnp.cos(ang), jnp.sin(ang)

def apply_grid_rope(x, cos, sin):
    B, L, n, _ = x.shape
    quarter = HEAD_DIM // 4
    xs = x.astype(F32).reshape(B, L, n, 2, 2, quarter)
    x1 = xs[..., 0, :]
    x2 = xs[..., 1, :]
    c = cos.reshape(1, L, 1, 2, quarter)
    s = sin.reshape(1, L, 1, 2, quarter)
    out = jnp.stack([x1 * c - x2 * s, x2 * c + x1 * s], axis=-2)
    return out.reshape(x.shape).astype(x.dtype)

def qkv_projection(h, w_qkv, q_g, k_g):
    B, L, _ = h.shape
    qkv = h @ w_qkv
    nq = N_HEADS * HEAD_DIM
    nk = N_KV_HEADS * HEAD_DIM
    q = qkv[..., :nq].reshape(B, L, N_HEADS, HEAD_DIM)
    k = qkv[..., nq:nq + nk].reshape(B, L, N_KV_HEADS, HEAD_DIM)
    v = qkv[..., nq + nk:].reshape(B, L, N_KV_HEADS, HEAD_DIM)
    return rms_norm(q, q_g), rms_norm(k, k_g), v

def block_attention(q, k, v):
    B, L, _, _ = q.shape
    nb = L // Q_BLOCK
    qb = q.reshape(B, nb, Q_BLOCK, N_KV_HEADS, Q_PER_KV, HEAD_DIM).transpose(1, 0, 2, 3, 4, 5)
    kf = k.astype(F32)
    vf = v.astype(F32)
    scale = HEAD_DIM ** -0.5

    def one_block(qblk):
        s = jnp.einsum('bqkgd,bskd->bkgqs', qblk.astype(F32), kf) * scale
        p = jax.nn.softmax(s, axis=-1)
        return jnp.einsum('bkgqs,bskd->bqkgd', p, vf).astype(v.dtype)

    o = lax.map(one_block, qb)
    return o.transpose(1, 0, 2, 3, 4, 5).reshape(B, L, N_HEADS * HEAD_DIM)

def attn_mixer_context(h, w_qkv, q_g, k_g, w_o):
    q, k, v = qkv_projection(h, w_qkv, q_g, k_g)
    o = block_attention(q, k, v)
    return o @ w_o, k, v

def attn_mixer_latent(h, k_ctx, v_ctx, w_qkv, q_g, k_g, w_o):
    q, k, v = qkv_projection(h, w_qkv, q_g, k_g)
    cos, sin = grid_rope_tables(h.shape[1])
    q = apply_grid_rope(q, cos, sin)
    k = apply_grid_rope(k, cos, sin)
    k_all = jnp.concatenate([k_ctx.astype(k.dtype), k], axis=1)
    v_all = jnp.concatenate([v_ctx.astype(v.dtype), v], axis=1)
    o = block_attention(q, k_all, v_all)
    return o @ w_o

def multi_scale_pool(h, w_pool, scale):
    B, L, D = h.shape
    hf = h.astype(F32)
    csum = jnp.concatenate([jnp.zeros((B, 1, D), F32), jnp.cumsum(hf, axis=1)], axis=1)
    csum = csum.reshape(B, L + 1, N_POOL_GROUPS, POOL_GROUP_DIM)
    win = jnp.array(POOL_WINDOWS, dtype=jnp.int32)
    left = win // 2
    right = win - left - 1
    t = jnp.arange(L, dtype=jnp.int32)[:, None]
    lo = jnp.maximum(t - left, 0)
    hi = jnp.minimum(t + right + 1, L)
    gi = jnp.arange(N_POOL_GROUPS)[None, :]
    window_sum = csum[:, hi, gi] - csum[:, lo, gi]
    mean = window_sum / (hi - lo).astype(F32)[None, :, :, None]
    diff = mean - hf.reshape(B, L, N_POOL_GROUPS, POOL_GROUP_DIM)
    out = jnp.einsum('blgc,gcd->blgd', diff, w_pool.astype(F32)).reshape(B, L, D)
    return (out * scale.astype(F32)).astype(h.dtype)

def hierarchical_moe(h, w_group, w_expert, w_gate, w_up, w_down):
    B, L, D = h.shape
    x = h.reshape(B * L, D)
    xf = x.astype(F32)
    group_logits = xf @ w_group.astype(F32)
    group_prob = jax.nn.softmax(group_logits, axis=-1)
    g_idx = jnp.argmax(group_logits, axis=-1)
    g_w = jnp.take_along_axis(group_prob, g_idx[:, None], axis=1)[:, 0]
    exp_logits = jnp.einsum('td,gde->tge', xf, w_expert.astype(F32))
    sel = jnp.take_along_axis(exp_logits, g_idx[:, None, None], axis=1)[:, 0]
    top_logit, top_j = lax.top_k(sel, TOP_K_IN_GROUP)
    weights = g_w[:, None] * jax.nn.softmax(top_logit, axis=-1)
    e_idx = g_idx[:, None] * EXPERTS_PER_GROUP + top_j
    combine = jnp.sum(jax.nn.one_hot(e_idx, N_EXPERTS, dtype=F32) * weights[..., None], axis=1)
    a = jnp.einsum('td,edf->tef', x, w_gate)
    b = jnp.einsum('td,edf->tef', x, w_up)
    hid = jax.nn.silu(a) * b * combine[:, :, None].astype(x.dtype)
    y = jnp.einsum('tef,efd->td', hid, w_down)
    return y.reshape(B, L, D)

def setup_inputs(seed: int = 0) -> dict:
    key = jax.random.key(seed)
    ks = jax.random.split(key, 24)

    def nrm(k, shape, s):
        return jax.random.normal(k, shape, F32) * s

    dq = (N_HEADS + 2 * N_KV_HEADS) * HEAD_DIM
    return {
        "x_prompt": nrm(ks[0], (BATCH, SEQ, D_MODEL), 1.0),
        "x_sample": nrm(ks[1], (DEC_BATCH, DEC_SEQ, D_MODEL), 1.0),
        "c": nrm(ks[2], (DEC_BATCH, D_MODEL), 1.0),
        "cache_k": nrm(ks[3], (DEC_BATCH, N_ATTN_LAYERS, PAST_LEN, N_KV_HEADS, HEAD_DIM), 1.0),
        "cache_v": nrm(ks[4], (DEC_BATCH, N_ATTN_LAYERS, PAST_LEN, N_KV_HEADS, HEAD_DIM), 1.0),
        "c_ctx": nrm(ks[5], (D_MODEL,), 1.0),
        "norm_mix_g": 1.0 + nrm(ks[6], (DEPTH, D_MODEL), 0.02),
        "norm_ffn_g": 1.0 + nrm(ks[7], (DEPTH, D_MODEL), 0.02),
        "ada_w": nrm(ks[8], (DEPTH, D_MODEL, N_MOD * D_MODEL), D_MODEL ** -0.5),
        "ada_b": nrm(ks[9], (DEPTH, N_MOD * D_MODEL), 0.02),
        "attn_w_qkv": nrm(ks[10], (N_ATTN_LAYERS, D_MODEL, dq), D_MODEL ** -0.5),
        "attn_q_norm": 1.0 + nrm(ks[11], (N_ATTN_LAYERS, HEAD_DIM), 0.02),
        "attn_k_norm": 1.0 + nrm(ks[12], (N_ATTN_LAYERS, HEAD_DIM), 0.02),
        "attn_w_o": nrm(ks[13], (N_ATTN_LAYERS, N_HEADS * HEAD_DIM, D_MODEL), (N_HEADS * HEAD_DIM) ** -0.5),
        "pool_w": nrm(ks[14], (N_POOL_LAYERS, N_POOL_GROUPS, POOL_GROUP_DIM, POOL_GROUP_DIM), POOL_GROUP_DIM ** -0.5),
        "pool_scale": 1.0 + nrm(ks[15], (N_POOL_LAYERS, D_MODEL), 0.1),
        "moe_w_group": nrm(ks[16], (DEPTH, D_MODEL, N_EXPERT_GROUPS), D_MODEL ** -0.5),
        "moe_w_expert": nrm(ks[17], (DEPTH, N_EXPERT_GROUPS, D_MODEL, EXPERTS_PER_GROUP), D_MODEL ** -0.5),
        "moe_w_gate": nrm(ks[18], (DEPTH, N_EXPERTS, D_MODEL, D_EXPERT), D_MODEL ** -0.5),
        "moe_w_up": nrm(ks[19], (DEPTH, N_EXPERTS, D_MODEL, D_EXPERT), D_MODEL ** -0.5),
        "moe_w_down": nrm(ks[20], (DEPTH, N_EXPERTS, D_EXPERT, D_MODEL), D_EXPERT ** -0.5),
    }

def reference(x_prompt, x_sample, c, cache_k, cache_v, c_ctx, norm_mix_g, norm_ffn_g, ada_w, ada_b,
              attn_w_qkv, attn_q_norm, attn_k_norm, attn_w_o, pool_w, pool_scale,
              moe_w_group, moe_w_expert, moe_w_gate, moe_w_up, moe_w_down):
    x = x_prompt
    cond_ctx = c_ctx[None, :]
    new_k_list = []
    new_v_list = []
    for l in range(DEPTH):
        sh1, sc1, g1, sh2, sc2, g2 = ada_modulation(cond_ctx, ada_w[l], ada_b[l])
        h = modulate(x, norm_mix_g[l], sh1, sc1)
        if l % N_MIXERS == 0:
            a = l // N_MIXERS
            m, k, v = attn_mixer_context(h, attn_w_qkv[a], attn_q_norm[a], attn_k_norm[a], attn_w_o[a])
            new_k_list.append(k)
            new_v_list.append(v)
        else:
            p = l // N_MIXERS
            m = multi_scale_pool(h, pool_w[p], pool_scale[p])
        x = x + g1 * m
        h = modulate(x, norm_ffn_g[l], sh2, sc2)
        x = x + g2 * hierarchical_moe(h, moe_w_group[l], moe_w_expert[l], moe_w_gate[l],
                                      moe_w_up[l], moe_w_down[l])
    y_prompt = x
    new_k = jnp.stack(new_k_list, axis=1)
    new_v = jnp.stack(new_v_list, axis=1)

    x = x_sample
    for l in range(DEPTH):
        sh1, sc1, g1, sh2, sc2, g2 = ada_modulation(c, ada_w[l], ada_b[l])
        h = modulate(x, norm_mix_g[l], sh1, sc1)
        if l % N_MIXERS == 0:
            a = l // N_MIXERS
            m = attn_mixer_latent(h, cache_k[:, a], cache_v[:, a], attn_w_qkv[a], attn_q_norm[a],
                                  attn_k_norm[a], attn_w_o[a])
        else:
            p = l // N_MIXERS
            m = multi_scale_pool(h, pool_w[p], pool_scale[p])
        x = x + g1 * m
        h = modulate(x, norm_ffn_g[l], sh2, sc2)
        x = x + g2 * hierarchical_moe(h, moe_w_group[l], moe_w_expert[l], moe_w_gate[l],
                                      moe_w_up[l], moe_w_down[l])
    y_sample = x
    return (y_prompt, y_sample, new_k, new_v)


_drawn_inputs = setup_inputs


def setup_inputs(seed=0):
    import zlib

    import numpy as np

    out = dict(_drawn_inputs(seed))
    spreads = {}
    factors = {'attn_q_norm': 3.36}
    for name, (base, spread) in spreads.items():
        noise = np.random.default_rng([zlib.crc32(name.encode()), seed]).standard_normal(out[name].shape)
        drawn = base * np.exp(spread * noise) if base else spread * noise
        out[name] = __import__('jax').numpy.asarray(drawn.astype(out[name].dtype))
    for name, factor in factors.items():
        out[name] = (out[name] * factor).astype(out[name].dtype)
    return out
```

```python
from contextlib import ExitStack

import numpy as np

import concourse.bass as bass
from concourse import mybir

F32 = mybir.dt.float32
U32 = mybir.dt.uint32
ALU = mybir.AluOpType
ACT = mybir.ActivationFunctionType
AX = mybir.AxisListType

P = 128
D = 1024
KD = D // P
NTOK = 384
TT = NTOK // P
CTX = 128
HEADS, KVH, HD = 16, 4, 64
QKV = (HEADS + 2 * KVH) * HD
NORMED = (HEADS + KVH) * HD
KEYS = 512
NE, NG, EPG = 32, 4, 8
FE = 256
EPS = 1e-6
SCALE = HD ** -0.5
TC = 64
EXTRA = (2 * NTOK - 1) // TC
NT = NE + EXTRA
RING = 4
ACH = 512
NCH = 6 * D // ACH
NONE = 4096.0
NMOD = 6 * KD
CONDS = ((0, 0, CTX), (1, CTX, NTOK))

_COLS = {}
_n = 0
for _name, _w in (("ident", P), ("ones", P), ("upper", P), ("sel2", 2), ("rep", 2 * P), ("assign", 6),
                  ("half", 1), ("first", NE), ("index", NE), ("rev", NE), ("revg", NG), ("extra", EXTRA),
                  ("cos", 2 * HD), ("sin", 2 * HD)):
    _COLS[_name] = (_n, _w)
    _n += _w
NCONST = _n
WINDOWS = (2, 4, 8, 16)
PADW = 8 + CTX + 16 + (NTOK - CTX) + 8
SEGS = ((0, 8, CTX), (CTX, 8 + CTX + 16, NTOK - CTX))


def constants():
    c = np.zeros((P, NCONST), np.float32)

    def put(name, v):
        a, w = _COLS[name]
        c[:, a:a + w] = v

    p = np.arange(P)[:, None]
    put("ident", np.eye(P))
    put("ones", 1.0)
    put("upper", p < np.arange(P)[None, :])
    put("sel2", (p % 32) == np.arange(2)[None, :])
    put("rep", np.concatenate([np.repeat((p % 32) == j, P, 1) for j in range(2)], 1))
    put("assign", np.concatenate([k * NTOK + t * P + p for k in range(2) for t in range(TT)], 1))
    put("half", p // TC)
    put("first", np.arange(NE)[None, :] * TC)
    put("index", np.arange(NE)[None, :])
    put("rev", NE - np.arange(NE)[None, :])
    put("revg", NG - np.arange(NG)[None, :])
    put("extra", np.arange(EXTRA)[None, :])
    pos = np.arange(NTOK - CTX)
    axis = HD // 2
    inv = np.float32(10000.0) ** (-np.arange(0, axis, 2, dtype=np.float32) / np.float32(axis))
    ang = [(pos // 64)[:, None].astype(np.float32) * inv, (pos % 64)[:, None].astype(np.float32) * inv]
    cos = np.concatenate([np.cos(ang[0]), np.cos(ang[0]), np.cos(ang[1]), np.cos(ang[1])], 1)
    sin = np.concatenate([-np.sin(ang[0]), np.sin(ang[0]), -np.sin(ang[1]), np.sin(ang[1])], 1)
    put("cos", np.concatenate([cos[:P], cos[P:]], 1))
    put("sin", np.concatenate([sin[:P], sin[P:]], 1))
    return c


def window_counts():
    out = np.zeros((len(WINDOWS), NTOK), np.float32)
    for g, w in enumerate(WINDOWS):
        for first, n in ((0, CTX), (CTX, NTOK - CTX)):
            t = np.arange(n)
            out[g, first:first + n] = 1.0 / (np.minimum(t + w - w // 2, n) - np.maximum(t - w // 2, 0))
    return np.repeat(out.reshape(1, -1), P, 0)


class Chain:

    def __init__(self, eng, sem):
        self.eng, self.sem, self.n = eng, sem, 0

    def __call__(self, ins):
        self.n += 1
        ins.then_inc(self.sem, 1)
        self.eng.wait_ge(self.sem, self.n)


def build(nc, x_prompt, x_sample, c, cache_k, cache_v, c_ctx, norm_mix_g, norm_ffn_g, ada_w, ada_b,
          attn_w_qkv, attn_q_norm, attn_k_norm, attn_w_o, pool_w, pool_scale, moe_w_group, moe_w_expert,
          moe_w_gate, moe_w_up, moe_w_down, consts, counts, y_prompt, y_sample, new_k, new_v,
          rows_dram, res_dram, slots_dram):
    with ExitStack() as ctx:
        def sb(name, shape, dt=F32):
            return ctx.enter_context(nc.sbuf_tensor(name, shape, dt))

        def sem(name):
            return ctx.enter_context(nc.semaphore(name))

        ring = sb("ring", [P, RING, 3 * KD * FE])
        adaw = sb("adaw", [P, 2, KD, ACH])
        xT = sb("xT", [P, KD, NTOK])
        hT = sb("hT", [P, KD, NTOK])
        xtok = sb("xtok", [P, TT, D])
        qkv = sb("qkv", [P, TT, QKV])
        con = sb("con", [P, NCONST])
        rowsA = sb("rowsA", [56, P])
        rowsB = sb("rowsB", [96, P])
        gains = sb("gains", [P, 56])
        bias = sb("bias", [P, 2, NMOD])
        condT = sb("condT", [P, KD, 32])
        adas = sb("adas", [P, 4, ACH])
        mods = sb("mods", [P, 2, NMOD, 2])
        wr = sb("wr", [P, 2, KD, NG + NE])
        qg = sb("qg", [P, 2, HD])
        ss = sb("ss", [P, 64])
        rt = sb("rt", [P, 640])
        wts = sb("wts", [P, 2, TT])
        slot_ids = sb("slot_ids", [P, 6], U32)
        tab = sb("tab", [NT, 2 * TC])
        gidx = sb("gidx", [P, NT], U32)
        sidx = sb("sidx", [P, NT], U32)
        gcur = sb("gcur", [P, 2], U32)
        scur = sb("scur", [P, 2], U32)
        extra_e = sb("extra_e", [P, EXTRA], U32)

        def C(name):
            a, w = _COLS[name]
            return con[:, a:a + w]

        ident, ones, upper = C("ident"), C("ones"), C("upper")

        low = ring[:, 0:2, :].rearrange("p a b -> p (a b)")
        wqkv = low.rearrange("p (k n) -> p k n", k=KD)
        qT = low[:, 0:KD * NTOK].rearrange("p (k t) -> p k t", k=KD)
        o = KD * NTOK
        kT = low[:, o:o + 2 * KVH * KEYS].rearrange("p (a h t) -> p a h t", a=2, h=KVH)
        o += 2 * KVH * KEYS
        probs = low[:, o:o + 3 * NTOK].rearrange("p (a t) -> p a t", a=3)
        o += 3 * NTOK
        probsT = low[:, o:o + 2 * NTOK].rearrange("p (a t) -> p a t", a=2)
        o += 2 * NTOK
        cache = low[:, o:o + 2 * KVH * HD].rearrange("p (a n) -> p a n", a=2)
        wo = ring[:, 2:4, :].rearrange("p a b -> p (a b)")[:, 0:KD * D].rearrange("p (k n) -> p k n", k=KD)
        tmp = [xtok[:, :, :].rearrange("p t d -> p (t d)")[:, i * NORMED:(i + 1) * NORMED] for i in range(2)]

        free = qkv[:, :, :].rearrange("p t n -> p (t n)")
        xg = free[:, 0:1024].rearrange("p (b n) -> p b n", b=2)
        xgT = free[:, 1024:2048].rearrange("p (b n) -> p b n", b=2)
        gated = free[:, 2048:2304].rearrange("p (b n) -> p b n", b=2)
        hid = free[:, 2304:2560].rearrange("p (b n) -> p b n", b=2)
        hidT = free[:, 2560:2816].rearrange("p (b n) -> p b n", b=2)
        yout = free[:, 2816:3840].rearrange("p (b n) -> p b n", b=2)
        sq = free[:, 3200:3200 + 2 * NTOK].rearrange("p (b n) -> p b n", b=2)
        rstd = free[:, 3200 + 2 * NTOK:3200 + 3 * NTOK]
        rcount = free[:, 0:4 * NTOK].rearrange("p (g t) -> p g t", g=4)
        sums = free[:, 4 * NTOK:4 * NTOK + 4 * PADW].rearrange("p (a k t) -> p a k t", a=2, k=2)

        cc = adaw[:, :, :, :].rearrange("p a k n -> p (a k n)")
        yrow = cc[:, 0:TT * 2 * D].rearrange("p (t k d) -> p t k d", t=TT, k=2)
        bias2 = cc[:, TT * 2 * D:TT * 2 * D + D]
        padded = cc[:, 0:KD * PADW].rearrange("p (k t) -> p k t", k=KD)
        poolw = cc[:, 4096:4096 + 2048].rearrange("p (g k n) -> p g k n", g=4, k=2)
        gate2 = hT[:, :, :].rearrange("p k t -> p (k t)")[:, 0:2 * D].rearrange("p (c d) -> p c d", c=2)

        bank = [ctx.enter_context(nc.psum_tensor(f"bank{i}", [P, 512], F32)) for i in range(8)]

        s_const, s_rows, s_x, s_wo, s_cache, s_wr, s_qg, s_empty, s_pool, s_bias2, s_out = map(sem, (
            "s_const", "s_rows", "s_x", "s_wo", "s_cache", "s_wr", "s_qg", "s_empty", "s_pool", "s_bias2", "s_out"))
        s_wqkv = [sem(f"s_wqkv{n}") for n in range(3)]
        s_adaw = [sem(f"s_adaw{i}") for i in range(2)]
        act_order, pool_order, dve_order = sem("act_order"), sem("pool_order"), sem("dve_order")
        cond_zero, rows_mm, rows_read, cond_ready = map(sem, ("cond_zero", "rows_mm", "rows_read", "cond_ready"))
        ada_mm, ada_copied, ada_vec, mods_ready = map(sem, ("ada_mm", "ada_copied", "ada_vec", "mods_ready"))
        ss_ready, std_x, xn_ready = sem("ss_ready"), sem("std_x"), sem("xn_ready")
        ms_x, rstd_x = sem("ms_x"), sem("rstd_x")
        xt_mm, xt_copied, hn_mm, h_ready = map(sem, ("xt_mm", "xt_copied", "hn_mm", "h_ready"))
        qkv_mm, qkv_copied, qkv_sq, qk_ms, qk_std, qkv_done = map(sem, (
            "qkv_mm", "qkv_copied", "qkv_sq", "qk_ms", "qk_std", "qkv_done"))
        qk_summed = sem("qk_summed")
        keys_zero, qk_mm, qk_copied = map(sem, ("keys_zero", "qk_mm", "qk_copied"))
        sc_mm, sc_max, sc_exp, pt_mm, pt_copied, pv_mm, o_copied = map(sem, (
            "sc_mm", "sc_max", "sc_exp", "pt_mm", "pt_copied", "pv_mm", "o_copied"))
        ot_mm, ot_copied = sem("ot_mm"), sem("ot_copied")
        mix_mm = [sem(f"mix_mm{n}") for n in range(3)]
        x_new = [sem(f"x_new{n}") for n in range(3)]
        sq_ready = [sem(f"sq_ready{n}") for n in range(3)]
        st_mm = [sem(f"st_mm{n}") for n in range(3)]
        ms_ready = [sem(f"ms_ready{n}") for n in range(3)]
        std_ready = [sem(f"std_ready{n}") for n in range(3)]
        h_new = [sem(f"h_new{n}") for n in range(3)]
        pad_zero, diff_ready = sem("pad_zero"), sem("diff_ready")

        lg_mm, lg_read, gexp, apart, texp, picked = map(sem, ("lg_mm", "lg_read", "gexp", "apart", "texp", "picked"))
        cnt_mm, over_ready, over_mm, slots_ready = map(sem, ("cnt_mm", "over_ready", "over_mm", "slots_ready"))
        extra_ready = sem("extra_ready")
        hb_mm, hb_copied, s_rowsout, empty_set, s_slots, s_tab, tab_mm, idx_ready, xg_clear = map(sem, (
            "hb_mm", "hb_copied", "s_rowsout", "empty_set", "s_slots", "s_tab", "tab_mm", "idx_ready", "xg_clear"))
        s_w = [sem(f"s_w{b}") for b in range(RING)]
        s_xg = [sem(f"s_xg{b}") for b in range(2)]
        s_y = [sem(f"s_y{b}") for b in range(2)]

        def users(l, b, n):
            return l * ((NT - b + n - 1) // n)

        xg_mm, xgT_ready, gu_mm, silu_ready, hid_ready, hid_mm, hidT_ready, down_mm, y_ready = map(sem, (
            "xg_mm", "xgT_ready", "gu_mm", "silu_ready", "hid_ready", "hid_mm", "hidT_ready", "down_mm", "y_ready"))
        s_yrow, y_sum = sem("s_yrow"), sem("y_sum")
        x1_mm, x1_copied, g2_mm, g2_ready, fin_ready = map(sem, ("x1_mm", "x1_copied", "g2_mm", "g2_ready", "fin_ready"))

        AFTER_QKV = {g: 4 + g for g in range(9)}
        AFTER_HEAD = {4 * i + 2: 13 + i for i in range(11)}
        ITEMS = [(t, h) for t in (1, 2, 0) for h in range(HEADS)]
        QTILES = (1, 2, 0)

        block = ctx.enter_context(nc.Block())

        @block.sync
        def _(sp):
            sp.dma_start(con[:, :], consts).then_inc(s_const, 16)
            for i, v in enumerate((norm_mix_g, norm_ffn_g)):
                sp.dma_start(rowsA[16 * i:16 * i + 16, :], v.rearrange("l (k p) -> (l k) p", p=P)).then_inc(s_rows, 16)
            sp.dma_start(rowsA[32:40, :], pool_scale.rearrange("l (k p) -> (l k) p", p=P)).then_inc(s_rows, 16)
            sp.dma_start(rowsA[40:48, :], c_ctx.rearrange("(k p) -> k p", p=P)).then_inc(s_rows, 16)
            sp.dma_start(rowsA[48:56, :], c.rearrange("l (k p) -> (l k) p", p=P)).then_inc(s_rows, 16)
            sp.dma_start(rowsB[:, :], ada_b.rearrange("l (k p) -> (l k) p", p=P)).then_inc(s_rows, 16)

            def load_ada(i):
                if i >= 2:
                    sp.wait_ge(ada_mm, i - 1)
                l, n = i // NCH, i % NCH
                sp.dma_start(adaw[:, i % 2], ada_w[l].rearrange("(k p) n -> p k n", p=P)[:, :, n * ACH:(n + 1) * ACH])\
                  .then_inc(s_adaw[i % 2], 16)

            def load_expert(l, e, b):
                slot = ring[:, b, :]
                for i, w in enumerate((moe_w_gate, moe_w_up)):
                    sp.dma_start(slot[:, i * KD * FE:(i + 1) * KD * FE],
                                 w[l, bass.ds(e, 1)].rearrange("o (p k) f -> (o p) (k f)", k=KD)).then_inc(s_w[b], 16)
                sp.dma_start(slot[:, 2 * KD * FE:].rearrange("p (j n) -> p j n", j=2),
                             moe_w_down[l, bass.ds(e, 1)].rearrange("o (j p) d -> p (o j) d", p=P)).then_inc(s_w[b], 16)

            load_ada(0)
            load_ada(1)
            sp.dma_start(xtok[:, 0, :], x_prompt[0]).then_inc(s_x, 16)
            sp.dma_start(xtok[:, 1:3, :], x_sample[0].rearrange("(t p) d -> p t d", p=P)).then_inc(s_x, 16)
            load_ada(2)
            load_ada(3)
            for n in range(3):
                sp.dma_start(wqkv[:, :, n * 512:(n + 1) * 512],
                             attn_w_qkv[0].rearrange("(k p) n -> p k n", p=P)[:, :, n * 512:(n + 1) * 512])\
                  .then_inc(s_wqkv[n], 16)
            load_ada(4)
            load_ada(5)
            sp.dma_start(wo, attn_w_o[0].rearrange("(k p) n -> p k n", p=P)).then_inc(s_wo, 16)
            for i in range(6, 2 * NCH):
                load_ada(i)

            for l in range(2):
                for b in range(RING):
                    if l == 0:
                        if b < 2:
                            sp.wait_ge(pv_mm, len(ITEMS))
                        else:
                            sp.wait_ge(mix_mm[0], KD)
                    else:
                        sp.wait_ge(down_mm, NT - (NT - 1 - b) % RING)
                    load_expert(l, b, b)
                with sp.Fori(1, NE // RING) as r:
                    for b in range(RING):
                        sp.wait_ge(down_mm, l * NT + r * RING + (b - RING + 1))
                        load_expert(l, r * RING + b, b)
                sp.wait_ge(extra_ready, l + 1)
                for j in range(EXTRA):
                    s = NE + j
                    e = sp.value_load(extra_e[0:1, j:j + 1], min_val=0, max_val=NE - 1)
                    sp.wait_ge(down_mm, l * NT + s - RING + 1)
                    load_expert(l, e, s % RING)

        @block.gpsimd
        def _(pool):
            G = nc.gpsimd
            G.memset(condT[:, :, :], 0.0).then_inc(cond_zero, 1)
            pool.wait_ge(qkv_mm, 9)
            pool.dma_start(cache[:, 0, :], cache_k[0, 0].rearrange("t h d -> t (h d)")).then_inc(s_cache, 16)
            pool.dma_start(cache[:, 1, :], cache_v[0, 0].rearrange("t h d -> t (h d)")).then_inc(s_cache, 16)
            G.memset(kT[HD:P, 0], 0.0).then_inc(keys_zero, 1)
            G.memset(kT[0:HD, 1], 0.0).then_inc(keys_zero, 1)
            copies = 0
            row_limit, res_limit = pool.to_reg(2 * NTOK - 1), pool.to_reg(4 * NTOK - 1)

            for l in range(2):
                if l:
                    pool.wait_ge(tab_mm, 1)
                G.memset(tab[:, :], NONE).then_inc(empty_set, 1)
                pool.wait_ge(empty_set, l + 1)
                pool.dma_start(slots_dram[l], tab[:, 0:TC]).then_inc(s_empty, 16)
                if l == 0:
                    pool.wait_ge(ot_mm, 6)
                    pool.wait_ge(s_out, 32)
                else:
                    pool.wait_ge(diff_ready, 4)
                G.memset(xg, 0.0).then_inc(xg_clear, 1)
                pool.wait_ge(slots_ready, l * 6 + 6)
                pool.wait_ge(s_empty, 16 * (l + 1))
                for i in range(6):
                    pool.indirect_dma_start(
                        slots_dram[l].rearrange("a (b o) -> (a b) o", o=1),
                        bass.IndirectOffsetOnAxis(ap=slot_ids[:, i:i + 1], axis=0),
                        C("assign")[:, i:i + 1], None, bounds_check=NT * TC - 1, oob_is_err=False)\
                        .then_inc(s_slots, 16)
                pool.wait_ge(s_slots, l * 96 + 96)
                for i in range(2):
                    pool.dma_start(tab[:, i * TC:(i + 1) * TC], slots_dram[l]).then_inc(s_tab, 16)
                pool.wait_ge(idx_ready, l * 2 + 2)
                pool.wait_ge(xg_clear, l + 1)
                pool.wait_ge(s_rowsout, l * 48 + 16 * TT)
                rows = rows_dram[l].rearrange("t (a n) -> (t a) n", a=2)
                res = res_dram[l].rearrange("t (a n) -> (t a) n", a=2)

                def gather(s, b, n):
                    G.tensor_copy(gcur[:, b:b + 1], gidx[:, bass.ds(s, 1)]).then_inc(pool_order, 1)
                    pool.wait_ge(pool_order, n + 1)
                    pool.reg_alu(row_limit, row_limit, 0, ALU.max)
                    pool.indirect_dma_start(
                        xg[:, b], None, rows, bass.IndirectOffsetOnAxis(ap=gcur[:, b:b + 1], axis=0),
                        bounds_check=row_limit, oob_is_err=False).then_inc(s_xg[b], 16)

                def scatter(s, b, n, old):
                    if old:
                        pool.wait_ge(s_y[b], s * 8 + (16 * users(l, b, 2) - 8 * b))
                    G.tensor_copy(scur[:, b:b + 1], sidx[:, bass.ds(s, 1)]).then_inc(pool_order, 1)
                    pool.wait_ge(pool_order, n + 1)
                    pool.wait_ge(y_ready, l * NT + s + 1)
                    pool.reg_alu(res_limit, res_limit, 0, ALU.max)
                    pool.indirect_dma_start(
                        res, bass.IndirectOffsetOnAxis(ap=scur[:, b:b + 1], axis=0),
                        yout[:, b], None, bounds_check=res_limit, oob_is_err=False).then_inc(s_y[b], 16)

                def step(s, b, n, more=True, old=True):
                    if more:
                        pool.wait_ge(xg_mm, l * NT + s + 1)
                        gather(s + 2, b, n)
                        n = n + 1
                    scatter(s, b, n, old)

                gather(0, 0, copies)
                gather(1, 1, copies + 1)
                step(0, 0, copies + 2, old=False)
                step(1, 1, copies + 4, old=False)
                copies += 6
                loops = (NT - 4) // 2
                with pool.Fori(0, loops) as r:
                    for b in range(2):
                        step(r * 2 + (2 + b), b, r * 4 + (copies + 2 * b))
                copies += 4 * loops
                for s in range(2 + 2 * loops, NT):
                    more = s + 2 < NT
                    step(s, s % 2, copies, more)
                    copies += 2 if more else 1
                for b in range(2):
                    pool.wait_ge(s_y[b], 16 * users(l + 1, b, 2))
                if l == 0:
                    pool.wait_ge(ada_mm, 2 * NCH)
                else:
                    pool.wait_ge(mix_mm[2], KD)
                for t in range(TT):
                    for k in range(2):
                        pool.dma_start(yrow[:, t, k], res_dram[l][k * NTOK + t * P:k * NTOK + (t + 1) * P, :])\
                            .then_inc(s_yrow, 16)
                if l == 0:
                    pool.dma_start(rcount, counts.rearrange("p (g t) -> p g t", g=4)).then_inc(s_pool, 16)
                    pool.wait_ge(mix_mm[1], KD)
                    G.memset(padded, 0.0).then_inc(pad_zero, 1)
                    pool.dma_start(poolw, pool_w[0].rearrange("g (k p) n -> p g k n", p=P)).then_inc(s_pool, 16)
            pool.wait_ge(s_out, 32 + 16 * TT)

        @block.scalar
        def _(act):
            A = nc.scalar
            act.dma_start(qg[:, 0, :], attn_q_norm[0:1, :].to_broadcast([P, HD])).then_inc(s_qg, 16)
            act.dma_start(qg[:, 1, :], attn_k_norm[0:1, :].to_broadcast([P, HD])).then_inc(s_qg, 16)
            for l in range(2):
                act.dma_start(wr[:, l, :, 0:NG], moe_w_group[l].rearrange("(k p) g -> p k g", p=P)).then_inc(s_wr, 16)
                for g in range(NG):
                    act.dma_start(wr[:, l, :, NG + g * EPG:NG + (g + 1) * EPG],
                                  moe_w_expert[l, g].rearrange("(k p) e -> p k e", p=P)).then_inc(s_wr, 16)
            act.wait_ge(rows_read, 1)
            act.wait_ge(cond_zero, 1)
            for i in range(2):
                A.activation(condT[:, :, i], gains[:, 40 + 8 * i:48 + 8 * i], ACT.Silu).then_inc(cond_ready, 1)
            act.wait_ge(s_x, 32)
            for t in range(TT):
                A.activation(free[:, t * D:(t + 1) * D], xtok[:, t, :], ACT.Square,
                             accum_out=ss[:, t:t + 1]).then_inc(ss_ready, 1)
            act.wait_ge(ms_x, 1)
            A.activation(ss[:, 4:7], ss[:, 8:11], ACT.Sqrt).then_inc(std_x, 1)

            def ada_copy(i):
                act.wait_ge(ada_mm, i + 1)
                if i >= 4:
                    act.wait_ge(ada_vec, i - 3)
                A.activation(adas[:, i % 4, :], bank[i % 2][:, :], ACT.Copy).then_inc(ada_copied, 1)

            for n in range(6):
                act.wait_ge(xt_mm, n + 1)
                t, q = n // 2, n % 2
                A.activation(xT[:, 4 * q:4 * q + 4, t * P:(t + 1) * P],
                             bank[4 + n % 2][:, :].rearrange("p (k t) -> p k t", k=4), ACT.Copy).then_inc(xt_copied, 1)
            for i in range(4):
                ada_copy(i)
            for g in range(9):
                t, n = QTILES[g // 3], g % 3
                act.wait_ge(qkv_mm, g + 1)
                b = bank[5 + g % 3]
                A.activation(qkv[:, t, n * 512:(n + 1) * 512], b[:, :], ACT.Copy).then_inc(qkv_copied, 1)
                w = min(512, NORMED - n * 512)
                if g >= 3:
                    act.wait_ge(qk_summed, g // 3)
                else:
                    act.wait_ge(xn_ready, TT)
                    act.wait_ge(hn_mm, KD)
                A.activation(tmp[0][:, n * 512:n * 512 + w], b[:, 0:w], ACT.Square).then_inc(qkv_sq, 1)
                if n == 2:
                    act.wait_ge(qk_ms, g // 3 + 1)
                    A.activation(ss[:, 40:60], ss[:, 20:40], ACT.Sqrt).then_inc(qk_std, 1)
                ada_copy(AFTER_QKV[g])
            act.wait_ge(qkv_done, 3)
            act.dma_start(new_k[0, 0].rearrange("t h d -> t (h d)"), qkv[:, 0, HEADS * HD:NORMED]).then_inc(s_out, 16)
            act.dma_start(new_v[0, 0].rearrange("t h d -> t (h d)"), qkv[:, 0, NORMED:QKV]).then_inc(s_out, 16)
            for i, (t, h) in enumerate(ITEMS):
                nk = P if t == 0 else 3 * P
                act.wait_ge(sc_max, i + 1)
                if i >= 3:
                    act.wait_ge(pt_mm, i - 2)
                A.activation(probs[:, i % 3, 0:nk], bank[3 + i % 2][:, 0:nk], ACT.Exp,
                             bias=ss[:, 60 + i % 2:61 + i % 2], scale=SCALE, accum_out=rt[:, i:i + 1]).then_inc(sc_exp, 1)
                if i in AFTER_HEAD:
                    ada_copy(AFTER_HEAD[i])

            def norm_act(n):
                for k in range(KD):
                    act.wait_ge(x_new[n], 2 * (k + 1))
                    if k >= 2:
                        act.wait_ge(st_mm[n], k - 1)
                    A.activation(sq[:, k % 2], xT[:, k, :], ACT.Square).then_inc(sq_ready[n], 1)
                act.wait_ge(ms_ready[n], 1)
                A.activation(rstd, rstd, ACT.Sqrt).then_inc(std_ready[n], 1)

            for l in range(2):
                if l:
                    norm_act(1)
                norm_act(2 * l)
                act.wait_ge(lg_read, l + 1)
                A.activation(rt[:, 112:124], rt[:, 112:124], ACT.Exp).then_inc(gexp, 1)
                for n in range(6):
                    t, q = n // 2, n % 2
                    act.wait_ge(hb_mm, l * 6 + n + 1)
                    A.activation(xtok[:, t, :].rearrange("p (k q) -> p q k", k=KD)[:, 64 * q:64 * q + 64, :],
                                 bank[4 + n % 2][:, :].rearrange("p (q k) -> p q k", k=KD), ACT.Copy)\
                        .then_inc(hb_copied, 1)
                    if q:
                        act.wait_ge(hb_copied, l * 6 + n + 1)
                        act.dma_start(rows_dram[l][t * P:(t + 1) * P, :], xtok[:, t, :]).then_inc(s_rowsout, 16)
                act.wait_ge(apart, l + 1)
                A.activation(rt[:, 136:139], rt[:, 136:139], ACT.Exp).then_inc(texp, 1)
                if l == 1:
                    act.wait_ge(mix_mm[2], KD)
                    act.dma_start(bias2, ada_b[1:2, 5 * D:6 * D].to_broadcast([P, D])).then_inc(s_bias2, 16)
                    act.wait_ge(s_rowsout, 48 + 16 * TT)
                    for n in range(6):
                        t, q = n // 2, n % 2
                        act.wait_ge(x1_mm, n + 1)
                        A.activation(xtok[:, t, q * 512:(q + 1) * 512], bank[6 + n % 2][:, :], ACT.Copy)\
                            .then_inc(x1_copied, 1)

                def silu(s, p, old=True):
                    act.wait_ge(gu_mm, l * NT + s + 1)
                    if old:
                        act.wait_ge(hid_ready, l * NT + s - 1)
                    A.activation(gated[:, p], bank[p][:, 0:P], ACT.Silu).then_inc(silu_ready, 1)

                def results(s, p, old=True):
                    act.wait_ge(down_mm, l * NT + s + 1)
                    if old:
                        act.wait_ge(s_y[p], s * 8 + (16 * users(l, p, 2) - 8 * p))
                    A.activation(yout[:, p], bank[4 + p][:, :], ACT.Copy).then_inc(y_ready, 1)

                silu(0, 0, old=False)
                for s in (1, 2):
                    silu(s, s % 2, old=s > 1)
                    results(s - 1, (s - 1) % 2, old=False)
                loops = (NT - 3) // 2
                with act.Fori(0, loops) as r:
                    for b in range(2):
                        silu(r * 2 + (3 + b), 1 - b)
                        results(r * 2 + (2 + b), b)
                for s in range(3 + 2 * loops, NT):
                    silu(s, s % 2)
                    results(s - 1, (s - 1) % 2)
                results(NT - 1, (NT - 1) % 2)
            for t in range(TT):
                act.wait_ge(fin_ready, t + 1)
                act.dma_start(y_prompt[0] if t == 0 else y_sample[0, (t - 1) * P:t * P, :], xtok[:, t, :]).then_inc(s_out, 16)
            act.wait_ge(s_out, 32 + 16 * TT)

        @block.vector
        def _(dve):
            V = nc.vector
            order = Chain(dve, dve_order)
            dve.wait_ge(rows_mm, 1)
            V.tensor_copy(gains[:, :], bank[3][:, 0:56]).then_inc(rows_read, 1)
            V.tensor_copy(bias[:, :, :].rearrange("p l m -> p (l m)"), bank[3][:, 64:160]).then_inc(rows_read, 1)
            dve.wait_ge(rows_read, 2)
            dve.wait_ge(ss_ready, TT)
            V.tensor_scalar(ss[:, 8:11], ss[:, 0:3], 1.0 / D, EPS, ALU.mult, ALU.add).then_inc(ms_x, 1)
            dve.wait_ge(std_x, 1)
            order(V.reciprocal(ss[:, 12:15], ss[:, 4:7]))
            dve.wait_ge(xt_mm, 6)
            for t in range(TT):
                V.tensor_scalar(xtok[:, t, :], xtok[:, t, :], ss[:, 12 + t:13 + t], None, ALU.mult).then_inc(xn_ready, 1)

            def modulation(l, a, b):
                cols = bank[2][:, l * 2 * NMOD + 2 * a * KD:l * 2 * NMOD + 2 * b * KD].rearrange("p (m c) -> p m c", c=2)
                m = mods[:, l, a * KD:b * KD, :]
                order(V.tensor_tensor(m, cols, bias[:, l, a * KD:b * KD].unsqueeze(2).to_broadcast([P, (b - a) * KD, 2]),
                                      ALU.add))
                for i, first in ((1, 8 * l), (4, 16 + 8 * l)):
                    if a <= i < b:
                        m = mods[:, l, i * KD:(i + 1) * KD, :]
                        order(V.tensor_scalar(m, m, 1.0, None, ALU.add))
                        order(V.tensor_tensor(m, m, gains[:, first:first + KD].unsqueeze(2).to_broadcast([P, KD, 2]),
                                              ALU.mult))

            def mod(l, i, k, cond):
                return mods[:, l, i * KD + k, cond:cond + 1]

            dve.wait_ge(ada_vec, 4)
            modulation(0, 0, 2)
            V.memset(ss[:, 15:16], 0.0).then_inc(mods_ready, 1)
            for k in range(KD):
                dve.wait_ge(hn_mm, k + 1)
                for cond, a, b in CONDS:
                    V.tensor_scalar(hT[:, k, a:b], bank[5 + k % 3][:, a:b], mod(0, 1, k, cond), mod(0, 0, k, cond),
                                    ALU.mult, ALU.add).then_inc(h_ready, 1)
            dve.wait_ge(s_qg, 32)
            dve.wait_ge(s_const, 16)
            for g in range(3):
                t = QTILES[g]
                dve.wait_ge(qkv_sq, 3 * g + 3)
                ins = V.tensor_reduce(ss[:, 20:40], tmp[0].rearrange("p (h d) -> p h d", d=HD), AX.X, ALU.add)
                ins.then_inc(qk_summed, 1)
                dve.wait_ge(qk_summed, g + 1)
                V.tensor_scalar(ss[:, 20:40], ss[:, 20:40], 1.0 / HD, EPS, ALU.mult, ALU.add).then_inc(qk_ms, 1)
                dve.wait_ge(qk_std, g + 1)
                order(V.reciprocal(ss[:, 20:40], ss[:, 40:60]))
                qk = qkv[:, t, 0:NORMED].rearrange("p (h d) -> p h d", d=HD)
                dve.wait_ge(qkv_copied, 3 * g + 3)
                order(V.tensor_tensor(qk, qk, ss[:, 20:40].unsqueeze(2).to_broadcast([P, 20, HD]), ALU.mult))
                for i, a, b in ((0, 0, HEADS), (1, HEADS, HEADS + KVH)):
                    last = V.tensor_tensor(qk[:, a:b], qk[:, a:b], qg[:, i, :].unsqueeze(1).to_broadcast([P, b - a, HD]),
                                           ALU.mult)
                    if i == 0 or t:
                        order(last)
                if t:
                    cos = C("cos")[:, (t - 1) * HD:t * HD].unsqueeze(1).to_broadcast([P, 20, HD])
                    sin = C("sin")[:, (t - 1) * HD:t * HD]
                    for a in range(4):
                        src = a ^ 1
                        order(V.tensor_tensor(
                            tmp[1].rearrange("p (h a d) -> p h a d", a=4, d=HD // 4)[:, :, a],
                            qkv[:, t, 0:NORMED].rearrange("p (h a d) -> p h a d", a=4, d=HD // 4)[:, :, src],
                            sin[:, a * 16:(a + 1) * 16].unsqueeze(1).to_broadcast([P, 20, HD // 4]), ALU.mult))
                    order(V.tensor_tensor(qk, qk, cos, ALU.mult))
                    last = V.tensor_tensor(qk, qk, tmp[1].rearrange("p (h d) -> p h d", d=HD), ALU.add)
                last.then_inc(qkv_done, 1)
            for n in range(6):
                dve.wait_ge(qk_mm, n + 1)
                t, q = n // 2, n % 2
                V.tensor_copy(qT[:, 4 * q:4 * q + 4, t * P:(t + 1) * P],
                              bank[3 + n % 2][:, :].rearrange("p (k t) -> p k t", k=4)).then_inc(qk_copied, 1)
            dve.wait_ge(keys_zero, 2)
            for n in range(4):
                dve.wait_ge(qk_mm, 7 + n)
                b = bank[3 + n % 2][:, 0:2 * P].rearrange("p (k t) -> p k t", k=2)
                for i, (parity, kv) in enumerate(((0, 0), (1, 0), (0, 1), (1, 1))):
                    last = V.tensor_copy(kT[64 * parity:64 * parity + 64, parity, kv::2, n * P:(n + 1) * P],
                                         b[64 * kv:64 * kv + 64])
                last.then_inc(qk_copied, 1)
            for i in range(len(ITEMS) + 2):
                if i < len(ITEMS):
                    t, h = ITEMS[i]
                    nk = P if t == 0 else 3 * P
                    dve.wait_ge(sc_mm, i + 1)
                    if i >= 2:
                        dve.wait_ge(sc_exp, i - 1)
                    order(V.tensor_reduce(ss[:, 16 + i % 2:17 + i % 2], bank[3 + i % 2][:, 0:nk], AX.X, ALU.max))
                    V.tensor_scalar(ss[:, 60 + i % 2:61 + i % 2], ss[:, 16 + i % 2:17 + i % 2], -SCALE, None, ALU.mult).then_inc(sc_max, 1)
                if 1 <= i <= len(ITEMS):
                    nk = P if ITEMS[i - 1][0] == 0 else 3 * P
                    dve.wait_ge(pt_mm, i)
                    if i >= 3:
                        dve.wait_ge(pv_mm, i - 2)
                    V.tensor_copy(probsT[:, (i - 1) % 2, 0:nk], bank[5 + (i - 1) % 2][:, 0:nk]).then_inc(pt_copied, 1)
                if i >= 2 and (i - 2) % 8 == 7:
                    j = i - 2
                    t, h = ITEMS[j]
                    dve.wait_ge(pv_mm, j + 1)
                    order(V.reciprocal(rt[:, 64:72], rt[:, j - 7:j + 1]))
                    V.tensor_tensor(qkv[:, t, (h - 7) * HD:(h + 1) * HD].rearrange("p (h d) -> p h d", d=HD),
                                    bank[7][:, :].rearrange("p (h d) -> p h d", d=HD),
                                    rt[:, 64:72].unsqueeze(2).to_broadcast([P, 8, HD]), ALU.mult).then_inc(o_copied, 1)
            for n in range(6):
                dve.wait_ge(ot_mm, n + 1)
                t, q = QTILES[n // 2], n % 2
                V.tensor_copy(hT[:, 4 * q:4 * q + 4, t * P:(t + 1) * P],
                              bank[3 + n % 2][:, :].rearrange("p (k t) -> p k t", k=4)).then_inc(ot_copied, 1)
            dve.wait_ge(ada_vec, 2 * NCH)
            modulation(0, 2, 6)
            modulation(1, 0, 6)
            m = mods[:, 1, 2 * KD:3 * KD, :]
            order(V.tensor_tensor(m, m, gains[:, 32:40].unsqueeze(2).to_broadcast([P, KD, 2]), ALU.mult))

            def add_to_stream(n, l, i, base):
                for k in range(KD):
                    dve.wait_ge(mix_mm[n], k + 1)
                    for cond, a, b in CONDS:
                        V.scalar_tensor_tensor(xT[:, k, a:b], bank[base + k % 2][:, a:b], mod(l, i, k, cond),
                                               xT[:, k, a:b], ALU.mult, ALU.add).then_inc(x_new[n], 1)

            def norm_dve(n, l, scale, shift, places):
                dve.wait_ge(st_mm[n], KD)
                V.tensor_scalar(rstd, bank[6][:, 0:NTOK], 1.0 / D, EPS, ALU.mult, ALU.add).then_inc(ms_ready[n], 1)
                dve.wait_ge(std_ready[n], 1)
                order(V.reciprocal(rstd, rstd))
                for k in range(KD):
                    order(V.tensor_tensor(hT[:, k, :], xT[:, k, :], rstd, ALU.mult))
                    for cond, a, b in CONDS:
                        V.tensor_scalar(places(k, a, b), hT[:, k, a:b], mod(l, scale, k, cond), mod(l, shift, k, cond),
                                        ALU.mult, ALU.add).then_inc(h_new[n], 1)

            def pick(values, mark, rev, best, n):
                shape = [P, TT, n]
                order(V.tensor_reduce(best, values, AX.X, ALU.max))
                order(V.tensor_tensor(mark, values, best.unsqueeze(2).to_broadcast(shape), ALU.is_equal))
                order(V.tensor_tensor(mark, mark, rev.unsqueeze(1).to_broadcast(shape), ALU.mult))
                order(V.tensor_reduce(rt[:, 108:111], mark, AX.X, ALU.max))
                order(V.tensor_tensor(mark, mark, rt[:, 108:111].unsqueeze(2).to_broadcast(shape), ALU.is_equal))

            def router(l):
                lg = rt[:, 0:108].rearrange("p (t e) -> p t e", t=TT)
                e32 = [rt[:, 160 + 96 * i:256 + 96 * i].rearrange("p (t e) -> p t e", t=TT) for i in range(5)]
                masked, first, second, both, work = e32
                gbest, m1, m2 = rt[:, 140:143], rt[:, 144:147], rt[:, 148:151]
                ge, gmark, far = rt[:, 112:124], rt[:, 124:136].rearrange("p (t g) -> p t g", t=TT), rt[:, 136:139]
                dve.wait_ge(lg_mm, l + 1)
                order(V.tensor_copy(rt[:, 0:108], bank[7][:, 0:108]))
                pick(lg[:, :, 0:NG], gmark, C("revg"), gbest, NG)
                V.tensor_tensor(ge.rearrange("p (t g) -> p t g", t=TT), lg[:, :, 0:NG],
                                gbest.unsqueeze(2).to_broadcast([P, TT, NG]), ALU.subtract).then_inc(lg_read, 1)
                m4 = masked.rearrange("p t (g e) -> p t g e", g=NG)
                for t in range(TT):
                    order(V.tensor_tensor(m4[:, t], lg[:, t, NG:].rearrange("p (g e) -> p g e", g=NG),
                                          gmark[:, t].unsqueeze(2).to_broadcast([P, NG, EPG]), ALU.mult))
                order(V.tensor_scalar(gmark, gmark, 1e30, -1e30, ALU.mult, ALU.add))
                for t in range(TT):
                    order(V.tensor_tensor(m4[:, t], m4[:, t], gmark[:, t].unsqueeze(2).to_broadcast([P, NG, EPG]), ALU.add))
                pick(masked, first, C("rev"), m1, NE)
                order(V.scalar_tensor_tensor(masked, first, -2e30, masked, ALU.mult, ALU.add))
                pick(masked, second, C("rev"), m2, NE)
                V.tensor_tensor(far, m2, m1, ALU.subtract).then_inc(apart, 1)
                V.tensor_tensor(both, first, second, ALU.add).then_inc(picked, 1)
                dve.wait_ge(gexp, l + 1)
                dve.wait_ge(apart, l + 1)
                order(V.tensor_reduce(gbest, ge.rearrange("p (t g) -> p t g", t=TT), AX.X, ALU.add))
                dve.wait_ge(texp, l + 1)
                order(V.tensor_scalar(m1, far, 1.0, None, ALU.add))
                order(V.tensor_tensor(m1, m1, gbest, ALU.mult))
                order(V.reciprocal(wts[:, 0, :], m1))
                order(V.tensor_tensor(wts[:, 1, :], wts[:, 0, :], far, ALU.mult))
                dve.wait_ge(cnt_mm, l + 1)
                over, tile_n = rt[0:NE, 152:153], rt[0:NE, 153:154]
                order(V.tensor_copy(tile_n, bank[6][0:NE, 128:129]))
                order(V.tensor_scalar(over, tile_n, float(TC), None, ALU.is_gt))
                for j in range(2, NTOK // TC):
                    order(V.scalar_tensor_tensor(over, tile_n, float(TC * j), over, ALU.is_gt, ALU.add))
                V.tensor_scalar(work[0:NE].rearrange("p t e -> p (t e)")[:, 0:96], ones[0:NE, 0:96], over, None,
                                ALU.mult).then_inc(over_ready, 1)
                V.tensor_scalar(rt[0:NE, 112:144], ones[0:NE, 0:32], over, None, ALU.mult).then_inc(over_ready, 1)
                dve.wait_ge(over_mm, l + 1)
                jump = rt[:, 0:NE]
                order(V.tensor_tensor(jump, bank[7][:, 128:128 + NE], C("rev"), ALU.add))
                order(V.tensor_scalar(jump, jump, float(TC), -float(TC), ALU.mult, ALU.add))
                pos = bank[6][:, 0:96].rearrange("p (t e) -> p t e", t=TT)
                shape = [P, TT, NE]
                order(V.tensor_scalar(work, pos, float(TC), None, ALU.is_ge))
                order(V.tensor_tensor(work, work, jump.unsqueeze(1).to_broadcast(shape), ALU.mult))
                order(V.tensor_tensor(work, work, C("first").unsqueeze(1).to_broadcast(shape), ALU.add))
                order(V.tensor_tensor(work, work, pos, ALU.add))
                for k, mark in enumerate((first, second)):
                    order(V.tensor_tensor(mark, mark, work, ALU.mult))
                    order(V.tensor_reduce(rt[:, 36 + 3 * k:39 + 3 * k], mark, AX.X, ALU.add))
                V.tensor_copy(slot_ids[:, :], rt[:, 36:42]).then_inc(slots_ready, 6)
                count = rt[0:1, 160:160 + EXTRA * NE].rearrange("p (j e) -> p j e", j=EXTRA)
                order(V.tensor_copy(rt[0:1, 48:80], bank[7][0:1, 160:192]))
                order(V.tensor_tensor(count, rt[0:1, 48:80].unsqueeze(1).to_broadcast([1, EXTRA, NE]),
                                      C("extra")[0:1].unsqueeze(2).to_broadcast([1, EXTRA, NE]), ALU.is_le))
                order(V.tensor_reduce(rt[0:1, 80:80 + EXTRA], count, AX.X, ALU.add))
                order(V.tensor_scalar(rt[0:1, 80:80 + EXTRA], rt[0:1, 80:80 + EXTRA], float(NE - 1), None, ALU.min))
                V.tensor_copy(extra_e[0:1, :], rt[0:1, 80:80 + EXTRA]).then_inc(extra_ready, 1)
                dve.wait_ge(tab_mm, l + 1)
                name, at = rt[:, 160:160 + NT], rt[:, 256:256 + NT]
                order(V.tensor_copy(name, bank[3][:, 0:NT]))
                V.tensor_scalar(sidx[:, :], name, 2.0, C("half"), ALU.mult, ALU.add).then_inc(idx_ready, 1)
                order(V.tensor_scalar(at, name, float(NTOK), -float(NTOK), ALU.is_ge, ALU.mult))
                order(V.tensor_tensor(at, at, name, ALU.add))
                V.tensor_scalar(gidx[:, :], at, 2.0, C("half"), ALU.mult, ALU.add).then_inc(idx_ready, 1)

            def experts(l):
                def rows_T(s, p, old=True):
                    dve.wait_ge(xg_mm, l * NT + s + 1)
                    if old:
                        dve.wait_ge(gu_mm, l * NT + s - 1)
                    V.tensor_copy(xgT[:, p], bank[2][:, :]).then_inc(xgT_ready, 1)

                def hidden(s, p, old=True):
                    dve.wait_ge(silu_ready, l * NT + s + 1)
                    if old:
                        dve.wait_ge(hid_mm, l * NT + s - 1)
                    V.tensor_tensor(hid[:, p], bank[p][:, P:2 * P], gated[:, p], ALU.mult).then_inc(hid_ready, 1)

                def hidden_T(s, p, old=True):
                    dve.wait_ge(hid_mm, l * NT + s + 1)
                    if old:
                        dve.wait_ge(down_mm, l * NT + s - 1)
                    V.tensor_copy(hidT[:, p], bank[3][:, 0:P]).then_inc(hidT_ready, 1)

                rows_T(0, 0, old=False)
                rows_T(1, 1, old=False)
                hidden(0, 0, old=False)
                hidden_T(0, 0, old=False)
                rows_T(2, 0)
                hidden(1, 1, old=False)
                hidden_T(1, 1, old=False)
                loops = (NT - 3) // 2
                with dve.Fori(0, loops) as r:
                    for b in range(2):
                        rows_T(r * 2 + (3 + b), 1 - b)
                        hidden(r * 2 + (2 + b), b)
                        hidden_T(r * 2 + (2 + b), b)
                for s in range(2 + 2 * loops, NT):
                    if s + 1 < NT:
                        rows_T(s + 1, (s + 1) % 2)
                    hidden(s, s % 2)
                    hidden_T(s, s % 2)

            def combine(l):
                dve.wait_ge(s_yrow, l * 96 + 16 * 2 * TT)
                for t in range(TT):
                    y = yrow[:, t, 0]
                    order(V.tensor_scalar(y, y, wts[:, 0, t:t + 1], None, ALU.mult))
                    last = V.scalar_tensor_tensor(y, yrow[:, t, 1], wts[:, 1, t:t + 1], y, ALU.mult, ALU.add)
                    if l == 0:
                        last.then_inc(y_sum, 1)
                    else:
                        order(last)
                        order(V.tensor_tensor(y, y, gate2[:, 0 if t == 0 else 1], ALU.mult))
                        dve.wait_ge(x1_copied, 2 * t + 2)
                        V.tensor_tensor(xtok[:, t, :], y, xtok[:, t, :], ALU.add).then_inc(fin_ready, 1)

            def pooling():
                dve.wait_ge(s_pool, 32)
                for g, w in enumerate(WINDOWS):
                    src, n = padded[:, 2 * g:2 * g + 2], PADW
                    step = 1
                    while step < w:
                        dst = sums[:, step.bit_length() % 2]
                        n -= step
                        order(V.tensor_tensor(dst[:, :, 0:n], src[:, :, 0:n], src[:, :, step:step + n], ALU.add))
                        src, step = dst, 2 * step
                    for first, at, m in SEGS:
                        out = hT[:, 2 * g:2 * g + 2, first:first + m]
                        a = at - w // 2
                        order(V.tensor_tensor(out, src[:, :, a:a + m],
                                              rcount[:, g, first:first + m].unsqueeze(1).to_broadcast([P, 2, m]), ALU.mult))
                        last = V.tensor_tensor(out, out, padded[:, 2 * g:2 * g + 2, at:at + m], ALU.subtract)
                        if first == 0:
                            order(last)
                    last.then_inc(diff_ready, 1)

            add_to_stream(0, 0, 2, 3)
            norm_dve(0, 0, 4, 3, lambda k, a, b: hT[:, k, a:b])
            router(0)
            experts(0)
            combine(0)
            add_to_stream(1, 0, 5, 4)
            dve.wait_ge(pad_zero, 1)
            norm_dve(1, 1, 1, 0, lambda k, a, b: padded[:, k, (8 if a == 0 else SEGS[1][1]):(8 if a == 0 else SEGS[1][1]) + b - a])
            dve.wait_ge(h_new[1], 2 * KD)
            pooling()
            add_to_stream(2, 1, 2, 4)
            norm_dve(2, 1, 4, 3, lambda k, a, b: hT[:, k, a:b])
            router(1)
            dve.wait_ge(s_bias2, 16)
            for n in range(4):
                dve.wait_ge(g2_mm, n + 1)
                a = (n % 2) * 512
                V.tensor_tensor(gate2[:, n // 2, a:a + 512], bank[6 + n % 2][:, :], bias2[:, a:a + 512], ALU.add)\
                    .then_inc(g2_ready, 1)
            experts(1)
            dve.wait_ge(g2_ready, 4)
            combine(1)

        @block.tensor
        def _(pe):
            T = nc.tensor
            pe.wait_ge(s_const, 16)
            pe.wait_ge(s_rows, 96)
            T.transpose(bank[3][:, 0:56], rowsA[:, :], ident[0:56, 0:56])
            T.transpose(bank[3][:, 64:160], rowsB[:, :], ident[0:96, 0:96]).then_inc(rows_mm, 1)
            pe.wait_ge(s_x, 32)
            for n in range(6):
                t, q = n // 2, n % 2
                if n >= 2:
                    pe.wait_ge(xt_copied, n - 1)
                for k in range(4):
                    last = T.transpose(bank[4 + n % 2][:, k * P:(k + 1) * P],
                                       xtok[:, t, (4 * q + k) * P:(4 * q + k + 1) * P], ident)
                last.then_inc(xt_mm, 1)

            def ada(i):
                if i == 0:
                    pe.wait_ge(cond_ready, 2)
                if i >= 2:
                    pe.wait_ge(ada_copied, i - 1)
                pe.wait_ge(s_adaw[i % 2], 16 * (i // 2 + 1))
                for half in range(2):
                    for j in range(4):
                        k = 4 * half + j
                        last = T.matmul(bank[i % 2][32 * j:32 * j + 32, :], condT[:, k, :], adaw[:, i % 2, k, :],
                                        start=half == 0, stop=half == 1, skip_group_check=True)
                last.then_inc(ada_mm, 1)

            def ada_vectors(i):
                pe.wait_ge(ada_copied, i + 1)
                l, n = i // NCH, i % NCH
                for j in range(ACH // P):
                    at = l * 2 * NMOD + 2 * (n * ACH // P + j)
                    last = T.matmul(bank[2][:, at:at + 2], adas[:, i % 4, j * P:(j + 1) * P], C("sel2"),
                                    start=True, stop=True)
                last.then_inc(ada_vec, 1)

            for i in range(4):
                ada(i)
                if i:
                    ada_vectors(i - 1)
            ada_vectors(3)
            for k in range(KD):
                if k == 0:
                    pe.wait_ge(xn_ready, TT)
                    pe.wait_ge(xt_copied, 6)
                if k >= 3:
                    pe.wait_ge(h_ready, 2 * (k - 2))
                for t in range(TT):
                    last = T.transpose(bank[5 + k % 3][:, t * P:(t + 1) * P], xtok[:, t, k * P:(k + 1) * P], ident)
                last.then_inc(hn_mm, 1)
            pe.wait_ge(h_ready, 2 * KD)
            for g in range(9):
                t, n = QTILES[g // 3], g % 3
                pe.wait_ge(s_wqkv[n], 16)
                if g >= 3:
                    pe.wait_ge(qkv_sq, g - 2)
                for k in range(KD):
                    last = T.matmul(bank[5 + g % 3][:, :], hT[:, k, t * P:(t + 1) * P], wqkv[:, k, n * 512:(n + 1) * 512],
                                    start=k == 0, stop=k == KD - 1)
                last.then_inc(qkv_mm, 1)
                if g == 0:
                    pe.wait_ge(mods_ready, 1)
                ada(AFTER_QKV[g])
                if g:
                    ada_vectors(AFTER_QKV[g] - 1)
            ada_vectors(AFTER_QKV[8])
            pe.wait_ge(qkv_done, 3)
            for n in range(10):
                if n >= 2:
                    pe.wait_ge(qk_copied, n - 1)
                b = bank[3 + n % 2]
                if n < 6:
                    t, q = n // 2, n % 2
                    parts = [qkv[:, t, (4 * q + k) * P:(4 * q + k + 1) * P] for k in range(4)]
                else:
                    m = n - 6
                    if m == 1:
                        pe.wait_ge(s_cache, 32)
                    src = cache[:, 0, :] if m == 1 else qkv[:, (0, None, 1, 2)[m], HEADS * HD:NORMED]
                    parts = [src[:, k * P:(k + 1) * P] for k in range(2)]
                for k, part in enumerate(parts):
                    last = T.transpose(b[:, k * P:(k + 1) * P], part, ident)
                last.then_inc(qk_mm, 1)
            pe.wait_ge(qk_copied, 10)
            for i in range(len(ITEMS) + 2):
                if i < len(ITEMS):
                    t, h = ITEMS[i]
                    keys = slice(0, P) if t == 0 else slice(P, KEYS)
                    if i >= 2:
                        pe.wait_ge(sc_exp, i - 1)
                    T.matmul(bank[3 + i % 2][:, 0:keys.stop - keys.start], qT[:, h // 2, t * P:(t + 1) * P],
                             kT[:, h % 2, h // 4, keys], start=True, stop=True).then_inc(sc_mm, 1)
                if 1 <= i <= len(ITEMS):
                    j = i - 1
                    nb = 1 if ITEMS[j][0] == 0 else 3
                    pe.wait_ge(sc_exp, j + 1)
                    if j >= 2:
                        pe.wait_ge(pt_copied, j - 1)
                    for k in range(nb):
                        last = T.transpose(bank[5 + j % 2][:, k * P:(k + 1) * P], probs[:, j % 3, k * P:(k + 1) * P], ident)
                    last.then_inc(pt_mm, 1)
                if i >= 2:
                    j = i - 2
                    t, h = ITEMS[j]
                    vcols = slice(NORMED + h // 4 * HD, NORMED + (h // 4 + 1) * HD)
                    values = [qkv[:, 0, vcols]] if t == 0 else [cache[:, 1, h // 4 * HD:(h // 4 + 1) * HD],
                                                                qkv[:, 1, vcols], qkv[:, 2, vcols]]
                    pe.wait_ge(pt_copied, j + 1)
                    if j % 8 == 0 and j:
                        pe.wait_ge(o_copied, j // 8)
                    for k, v in enumerate(values):
                        last = T.matmul(bank[7][:, (h % 8) * HD:(h % 8 + 1) * HD], probsT[:, j % 2, k * P:(k + 1) * P], v,
                                        start=k == 0, stop=k == len(values) - 1)
                    last.then_inc(pv_mm, 1)
                if i in AFTER_HEAD:
                    ada(AFTER_HEAD[i])
                    if AFTER_HEAD[i] > 13:
                        ada_vectors(AFTER_HEAD[i] - 1)
            ada_vectors(2 * NCH - 1)
            pe.wait_ge(o_copied, 6)
            for n in range(6):
                if n >= 2:
                    pe.wait_ge(ot_copied, n - 1)
                t, q = QTILES[n // 2], n % 2
                for k in range(4):
                    last = T.transpose(bank[3 + n % 2][:, k * P:(k + 1) * P],
                                       qkv[:, t, (4 * q + k) * P:(4 * q + k + 1) * P], ident)
                last.then_inc(ot_mm, 1)
            pe.wait_ge(ot_copied, 6)
            pe.wait_ge(s_wo, 16)
            for d in range(KD):
                if d >= 2:
                    pe.wait_ge(x_new[0], 2 * (d - 1))
                for k in range(KD):
                    last = T.matmul(bank[3 + d % 2][:, 0:NTOK], wo[:, k, d * P:(d + 1) * P], hT[:, k, :],
                                    start=k == 0, stop=k == KD - 1)
                last.then_inc(mix_mm[0], 1)

            def norm_pe(n):
                for k in range(KD):
                    pe.wait_ge(sq_ready[n], k + 1)
                    T.matmul(bank[6][:, 0:NTOK], ones, sq[:, k % 2], start=k == 0, stop=k == KD - 1).then_inc(st_mm[n], 1)

            for l in range(2):
                norm_pe(2 * l)
                if l == 0:
                    pe.wait_ge(s_wr, 160)
                pe.wait_ge(h_new[2 * l], 2 * KD)
                for t in range(TT):
                    for k in range(KD):
                        last = T.matmul(bank[7][:, t * 36:(t + 1) * 36], hT[:, k, t * P:(t + 1) * P], wr[:, l, k, :],
                                        start=k == 0, stop=k == KD - 1)
                last.then_inc(lg_mm, 1)
                for n in range(6):
                    t, q = n // 2, n % 2
                    if n >= 2:
                        pe.wait_ge(hb_copied, l * 6 + n - 1)
                    for k in range(4):
                        last = T.transpose(bank[4 + n % 2][:, k * P:(k + 1) * P], hT[:, 4 * q + k, t * P:(t + 1) * P], ident)
                    last.then_inc(hb_mm, 1)
                pe.wait_ge(picked, l + 1)
                both = rt[:, 160 + 96 * 3:256 + 96 * 3].rearrange("p (t e) -> p t e", t=TT)
                for t in range(TT):
                    for j in range(t + 1):
                        T.matmul(bank[6][:, t * NE:(t + 1) * NE], upper if j == t else ones, both[:, j],
                                 start=j == 0, stop=j == t)
                for t in range(TT):
                    last = T.matmul(bank[6][0:NE, 128:129], both[:, t], ones[:, 0:1], start=t == 0, stop=t == TT - 1)
                last.then_inc(cnt_mm, 1)
                pe.wait_ge(over_ready, l * 2 + 2)
                parts = ((rt[0:NE, 160 + 96 * 4:256 + 96 * 4], 0, 96), (rt[0:NE, 112:144], 96, P))
                for lhs, a, b in parts:
                    T.matmul(bank[7][a:b, 128:128 + NE], lhs, upper[0:NE, 0:NE], start=True, stop=True)
                for m, sel in enumerate((upper, ident)):
                    last = T.matmul(bank[7][0:96, 160:160 + NE], parts[0][0], sel[0:NE, 0:NE], start=m == 0, stop=m == 1)
                last.then_inc(over_mm, 1)
                if l == 1:
                    pe.wait_ge(slots_ready, 6 + 6)
                    pe.wait_ge(extra_ready, 1 + 1)
                    for n in range(6):
                        t, q = n // 2, n % 2
                        if n >= 2:
                            pe.wait_ge(x1_copied, n - 1)
                        for k in range(4):
                            last = T.transpose(bank[6 + n % 2][:, k * P:(k + 1) * P], xT[:, 4 * q + k, t * P:(t + 1) * P], ident)
                        last.then_inc(x1_mm, 1)
                    pe.wait_ge(x1_copied, 6)
                pe.wait_ge(s_tab, l * 32 + 32)
                T.transpose(bank[3][:, 0:NT], tab[:, :], ident[0:NT, 0:NT]).then_inc(tab_mm, 1)
                if l == 1:
                    for n in range(4):
                        if n >= 2:
                            pe.wait_ge(g2_ready, n - 1)
                        T.matmul(bank[6 + n % 2][:, :], C("rep")[:, (n // 2) * P:(n // 2 + 1) * P],
                                 adas[:, (2 * NCH - 2 + n % 2) % 4, :], start=True, stop=True).then_inc(g2_mm, 1)
                pe.wait_ge(idx_ready, l * 2 + 2)

                def rows_T(s, p, old=True):
                    pe.wait_ge(s_xg[p], s * 8 + (16 * users(l, p, 2) + 16 - 8 * p))
                    if old:
                        pe.wait_ge(xgT_ready, l * NT + s)
                    for i in range(4):
                        last = T.transpose(bank[2][:, i * P:(i + 1) * P], xg[:, p, i * P:(i + 1) * P], ident)
                    last.then_inc(xg_mm, 1)

                def gate_up(s, p, b, old=True):
                    pe.wait_ge(xgT_ready, l * NT + s + 1)
                    pe.wait_ge(s_w[b], s * 12 + (48 * users(l, b, RING) + 48 - 12 * b))
                    if old:
                        pe.wait_ge(hid_ready, l * NT + s - 1)
                    w = ring[:, b, 0:2 * KD * FE].rearrange("p (g k f) -> p g k f", g=2, k=KD)
                    xk = xgT[:, p].rearrange("p (i a c) -> p i a c", i=4, a=2)
                    for k in range(KD):
                        for a in range(2):
                            last = T.matmul(bank[p][64 * a:64 * a + 64, 0:2 * P], xk[:, k % 4, k // 4],
                                            w[:, :, k, a * P:(a + 1) * P], start=k == 0, stop=k == KD - 1,
                                            skip_group_check=True)
                    last.then_inc(gu_mm, 1)

                def hidden_T(s, p, old=True):
                    pe.wait_ge(hid_ready, l * NT + s + 1)
                    if old:
                        pe.wait_ge(hidT_ready, l * NT + s)
                    T.transpose(bank[3][:, 0:P], hid[:, p], ident).then_inc(hid_mm, 1)

                def down(s, p, b, old=True):
                    pe.wait_ge(hidT_ready, l * NT + s + 1)
                    if old:
                        pe.wait_ge(y_ready, l * NT + s - 1)
                    w = ring[:, b, 2 * KD * FE:].rearrange("p (j n) -> p j n", j=2)
                    for j in range(2):
                        for a in range(2):
                            last = T.matmul(bank[4 + p][64 * a:64 * a + 64, :], hidT[:, p, 64 * j:64 * j + 64],
                                            w[:, j, a * 512:(a + 1) * 512], start=j == 0, stop=j == 1,
                                            skip_group_check=True)
                    last.then_inc(down_mm, 1)

                def step(s, q, more=True, old=2):
                    gate_up(s, q % 2, q, old=old >= 1)
                    if more:
                        rows_T(s + 1, (q + 1) % 2)
                    down(s - 1, (q + 1) % 2, (q + RING - 1) % RING, old=old >= 2)
                    hidden_T(s, q % 2)

                rows_T(0, 0, old=False)
                gate_up(0, 0, 0, old=False)
                rows_T(1, 1)
                hidden_T(0, 0, old=False)
                step(1, 1, old=0)
                step(2, 2, old=1)
                loops = (NT - 4) // RING
                with pe.Fori(0, loops) as r:
                    for q in range(RING):
                        step(r * RING + (3 + q), (3 + q) % RING)
                for s in range(3 + RING * loops, NT):
                    step(s, s % RING, more=s + 1 < NT)
                down(NT - 1, (NT - 1) % 2, (NT - 1) % RING)
                if l == 0:
                    pe.wait_ge(y_sum, TT)
                    pe.wait_ge(y_ready, NT)
                    for k in range(KD):
                        if k >= 2:
                            pe.wait_ge(x_new[1], 2 * (k - 1))
                        for t in range(TT):
                            last = T.transpose(bank[4 + k % 2][:, t * P:(t + 1) * P], yrow[:, t, 0, k * P:(k + 1) * P], ident)
                        last.then_inc(mix_mm[1], 1)
                    norm_pe(1)
                    pe.wait_ge(s_pool, 32)
                    pe.wait_ge(x_new[1], 2 * KD)
                    for k in range(KD):
                        g = k // 2
                        pe.wait_ge(diff_ready, g + 1)
                        if k >= 2:
                            pe.wait_ge(x_new[2], 2 * (k - 1))
                        for j in range(2):
                            last = T.matmul(bank[4 + k % 2][:, 0:NTOK], poolw[:, g, j, (k % 2) * P:(k % 2 + 1) * P],
                                            hT[:, 2 * g + j, :], start=j == 0, stop=j == 1)
                        last.then_inc(mix_mm[2], 1)


_INS = ["x_prompt", "x_sample", "c", "cache_k", "cache_v", "c_ctx", "norm_mix_g", "norm_ffn_g", "ada_w", "ada_b",
        "attn_w_qkv", "attn_q_norm", "attn_k_norm", "attn_w_o", "pool_w", "pool_scale", "moe_w_group",
        "moe_w_expert", "moe_w_gate", "moe_w_up", "moe_w_down"]
_OUTS = [(1, CTX, D), (1, NTOK - CTX, D), (1, 1, CTX, KVH, HD), (1, 1, CTX, KVH, HD)]


def kernel(**inputs):
    import concourse.bacc as bacc
    from concourse.bass_utils import run_bass_kernel_spmd

    nc = bacc.Bacc("TRN2", target_bir_lowering=False, num_devices=1)
    arrays = {f"in_{n}": np.ascontiguousarray(inputs[n]) for n in _INS}
    arrays["in_constants"] = constants()
    arrays["in_counts"] = window_counts()
    args = [nc.dram_tensor(n, a.shape, F32, kind="ExternalInput").ap() for n, a in arrays.items()]
    args += [nc.dram_tensor(f"out_{i}", s, F32, kind="ExternalOutput").ap() for i, s in enumerate(_OUTS)]
    args += [[nc.dram_tensor(f"{n}{l}", s, F32, kind="Internal").ap() for l in range(2)]
             for n, s in (("rows", (NTOK, D)), ("results", (2 * NTOK, D)), ("slots", (NT, TC)))]
    build(nc, *args)
    r = run_bass_kernel_spmd(nc, [arrays], core_ids=[0])
    return tuple(r.results[0][f"out_{i}"] for i in range(len(_OUTS)))
```

```python
from contextlib import ExitStack

import numpy as np

import concourse.bass as bass
from concourse import mybir

F32 = mybir.dt.float32
U32 = mybir.dt.uint32
ALU = mybir.AluOpType
ACT = mybir.ActivationFunctionType
AX = mybir.AxisListType

P = 128
D = 1024
KD = D // P
NTOK = 384
TT = NTOK // P
CTX = 128
HEADS, KVH, HD = 16, 4, 64
QKV = (HEADS + 2 * KVH) * HD
NORMED = (HEADS + KVH) * HD
KEYS = 512
NE, NG, EPG = 32, 4, 8
FE = 256
EPS = 1e-6
SCALE = HD ** -0.5
TC = 64
EXTRA = (2 * NTOK - 1) // TC
NT = NE + EXTRA
RING = 4
NBUF = 4
ACH = 512
NCH = 6 * D // ACH
NONE = 4096.0
NMOD = 6 * KD
CONDS = ((0, 0, CTX), (1, CTX, NTOK))

_COLS = {}
_n = 0
for _name, _w in (("ident", P), ("ones", P), ("upper", P), ("sel2", 2), ("rep", 2 * P), ("assign", 6),
                  ("half", 1), ("place", P), ("tiles", NT), ("first", NE), ("rev", NE), ("revg", NG), ("extra", EXTRA),
                  ("cos", 2 * HD), ("sin", 2 * HD)):
    _COLS[_name] = (_n, _w)
    _n += _w
NCONST = _n
WINDOWS = (2, 4, 8, 16)
PADW = 8 + CTX + 16 + (NTOK - CTX) + 8
SEGS = ((0, 8, CTX), (CTX, 8 + CTX + 16, NTOK - CTX))


def constants():
    c = np.zeros((P, NCONST), np.float32)

    def put(name, v):
        a, w = _COLS[name]
        c[:, a:a + w] = v

    p = np.arange(P)[:, None]
    put("ident", np.eye(P))
    put("ones", 1.0)
    put("upper", p < np.arange(P)[None, :])
    put("sel2", (p % 32) == np.arange(2)[None, :])
    put("rep", np.concatenate([np.repeat((p % 32) == j, P, 1) for j in range(2)], 1))
    put("assign", np.concatenate([k * NTOK + t * P + p for k in range(2) for t in range(TT)], 1) - NONE)
    put("half", 2 * NONE + p // TC)
    put("place", np.arange(P)[None, :] % TC)
    put("tiles", np.arange(NT)[None, :] * TC)
    put("first", np.arange(NE)[None, :] * TC)
    put("rev", NE - np.arange(NE)[None, :])
    put("revg", NG - np.arange(NG)[None, :])
    put("extra", np.arange(EXTRA)[None, :])
    pos = np.arange(NTOK - CTX)
    axis = HD // 2
    inv = np.float32(10000.0) ** (-np.arange(0, axis, 2, dtype=np.float32) / np.float32(axis))
    ang = [(pos // 64)[:, None].astype(np.float32) * inv, (pos % 64)[:, None].astype(np.float32) * inv]
    cos = np.concatenate([np.cos(ang[0]), np.cos(ang[0]), np.cos(ang[1]), np.cos(ang[1])], 1)
    sin = np.concatenate([-np.sin(ang[0]), np.sin(ang[0]), -np.sin(ang[1]), np.sin(ang[1])], 1)
    put("cos", np.concatenate([cos[:P], cos[P:]], 1))
    put("sin", np.concatenate([sin[:P], sin[P:]], 1))
    return c


def window_counts():
    out = np.zeros((len(WINDOWS), NTOK), np.float32)
    for g, w in enumerate(WINDOWS):
        for first, n in ((0, CTX), (CTX, NTOK - CTX)):
            t = np.arange(n)
            out[g, first:first + n] = 1.0 / (np.minimum(t + w - w // 2, n) - np.maximum(t - w // 2, 0))
    return np.repeat(out.reshape(1, -1), P, 0)


class Chain:

    def __init__(self, eng, sem, n=0):
        self.eng, self.sem, self.n = eng, sem, n

    def __call__(self, ins):
        self.n += 1
        ins.then_inc(self.sem, 1)
        self.eng.wait_ge(self.sem, self.n)


def build(nc, x_prompt, x_sample, c, cache_k, cache_v, c_ctx, norm_mix_g, norm_ffn_g, ada_w, ada_b,
          attn_w_qkv, attn_q_norm, attn_k_norm, attn_w_o, pool_w, pool_scale, moe_w_group, moe_w_expert,
          moe_w_gate, moe_w_up, moe_w_down, consts, counts, y_prompt, y_sample, new_k, new_v,
          rows_dram, res_dram):
    with ExitStack() as ctx:
        def sb(name, shape, dt=F32):
            return ctx.enter_context(nc.sbuf_tensor(name, shape, dt))

        def sem(name):
            return ctx.enter_context(nc.semaphore(name))

        ring = sb("ring", [P, RING, 3 * KD * FE])
        adaw = sb("adaw", [P, 2, KD, ACH])
        xT = sb("xT", [P, KD, NTOK])
        hT = sb("hT", [P, KD, NTOK])
        xtok = sb("xtok", [P, TT, D])
        qkv = sb("qkv", [P, TT, QKV])
        con = sb("con", [P, NCONST])
        rowsA = sb("rowsA", [56, P])
        rowsB = sb("rowsB", [96, P])
        gains = sb("gains", [P, 56])
        bias = sb("bias", [P, 2, NMOD])
        condT = sb("condT", [P, KD, 32])
        adas = sb("adas", [P, 4, ACH])
        mods = sb("mods", [P, 2, NMOD, 2])
        wr = sb("wr", [P, 2, KD, NG + NE])
        qg = sb("qg", [P, 2, HD])
        ss = sb("ss", [P, 64])
        rt = sb("rt", [P, 640])
        wts = sb("wts", [P, 2, TT])
        gidx = sb("gidx", [P, NT], U32)
        sidx = sb("sidx", [P, NT], U32)
        gcur = sb("gcur", [P, NBUF], U32)
        scur = sb("scur", [P, NBUF], U32)
        extra_e = sb("extra_e", [1, EXTRA + 1], U32)

        def C(name):
            a, w = _COLS[name]
            return con[:, a:a + w]

        ident, ones, upper = C("ident"), C("ones"), C("upper")

        low = ring[:, 0:2, :].rearrange("p a b -> p (a b)")
        wqkv = [low[:, n * KD * 512:(n + 1) * KD * 512].rearrange("p (k n) -> p k n", k=KD) for n in range(3)]
        qT = low[:, 0:KD * NTOK].rearrange("p (k t) -> p k t", k=KD)
        cache = low[:, KD * NTOK:KD * NTOK + 2 * KVH * HD].rearrange("p (a n) -> p a n", a=2)
        o = KD * 512
        kT = low[:, o:o + 2 * KVH * KEYS].rearrange("p (a h t) -> p a h t", a=2, h=KVH)
        o += 2 * KVH * KEYS
        probs = low[:, o:o + 3 * NTOK].rearrange("p (a t) -> p a t", a=3)
        o += 3 * NTOK
        probsT = low[:, o:o + 2 * NTOK].rearrange("p (a t) -> p a t", a=2)
        high = ring[:, 2:4, :].rearrange("p a b -> p (a b)")
        wo = high[:, 0:KD * D].rearrange("p (k n) -> p k n", k=KD)
        ada_place = [adaw[:, 0], adaw[:, 1], high[:, KD * D:].rearrange("p (k n) -> p k n", k=KD)]
        tmp = [xtok[:, :, :].rearrange("p t d -> p (t d)")[:, i * NORMED:(i + 1) * NORMED] for i in range(2)]

        free = qkv[:, :, :].rearrange("p t n -> p (t n)")
        xgT = free[:, 1536:2560].rearrange("p (b n) -> p b n", b=2)
        gated = free[:, 2560:2816].rearrange("p (b n) -> p b n", b=2)
        hid = free[:, 2816:3072].rearrange("p (b n) -> p b n", b=2)
        hidT = free[:, 3072:3328].rearrange("p (b n) -> p b n", b=2)
        sq = free[:, 3200:3200 + 2 * NTOK].rearrange("p (b n) -> p b n", b=2)
        rstd = free[:, 3200 + 2 * NTOK:3200 + 3 * NTOK]
        rcount = free[:, 0:4 * NTOK].rearrange("p (g t) -> p g t", g=4)
        sums = free[:, 4 * NTOK:4 * NTOK + 4 * PADW].rearrange("p (a k t) -> p a k t", a=2, k=2)

        cc = adaw[:, :, :, :].rearrange("p a k n -> p (a k n)")
        xg = cc[:, 0:2048].rearrange("p (b n) -> p b n", b=NBUF)
        yout = cc[:, 2048:4096].rearrange("p (b n) -> p b n", b=NBUF)
        yrow = cc[:, 0:TT * 2 * D].rearrange("p (t k d) -> p t k d", t=TT, k=2)
        bias2 = free[:, 0:D]
        padded = cc[:, 0:KD * PADW].rearrange("p (k t) -> p k t", k=KD)
        poolw = xtok[:, 0:2, :].rearrange("p t d -> p (t d)").rearrange("p (g k n) -> p g k n", g=4, k=2)
        gate2 = hT[:, :, :].rearrange("p k t -> p (k t)")[:, 0:2 * D].rearrange("p (c d) -> p c d", c=2)

        flat_h = hT[:, :, :].rearrange("p k t -> p (k t)")
        more_gu = cc[:, 4096:8192]
        more_down = [flat_h[:, 2 * D:3 * D], adas[:, 0:2, :].rearrange("p a n -> p (a n)")]
        at_place = flat_h[:, 0:6 * P].rearrange("p (i n) -> p i n", i=6)
        in_tile = flat_h[:, 6 * P:6 * P + 6 * NT].rearrange("p (i n) -> p i n", i=6)
        diag = flat_h[:, 1100:1100 + 6 * P].rearrange("p (i n) -> p i n", i=6)
        sums2 = cc[:, KD * PADW:(KD + 4) * PADW].rearrange("p (a k t) -> p a k t", a=2, k=2)

        bank = [ctx.enter_context(nc.psum_tensor(f"bank{i}", [P, 512], F32)) for i in range(8)]

        s_const, s_rows, s_x, s_wo, s_cache, s_wr, s_qg, s_pool, s_bias2, s_out = map(sem, (
            "s_const", "s_rows", "s_x", "s_wo", "s_cache", "s_wr", "s_qg", "s_pool", "s_bias2", "s_out"))
        s_wqkv = [sem(f"s_wqkv{n}") for n in range(3)]
        s_adaw = [sem(f"s_adaw{i}") for i in range(3)]
        pool_order, dve_order = sem("pool_order"), sem("dve_order")
        cond_zero, rows_mm, rows_read, cond_ready = map(sem, ("cond_zero", "rows_mm", "rows_read", "cond_ready"))
        ada_mm, ada_copied, ada_vec, mods_ready = map(sem, ("ada_mm", "ada_copied", "ada_vec", "mods_ready"))
        ss_ready, std_x, xn_ready = sem("ss_ready"), sem("std_x"), sem("xn_ready")
        ms_x = sem("ms_x")
        xt_mm, xt_copied, hn_mm, hn_copied, h_ready = map(sem, ("xt_mm", "xt_copied", "hn_mm", "hn_copied", "h_ready"))
        qkv_mm, qkv_copied, qkv_sq, qk_ms, qk_std, qkv_done = map(sem, (
            "qkv_mm", "qkv_copied", "qkv_sq", "qk_ms", "qk_std", "qkv_done"))
        qk_summed = sem("qk_summed")
        keys_zero, qk_mm, qk_copied, k_mm, k_copied = map(sem, ("keys_zero", "qk_mm", "qk_copied", "k_mm", "k_copied"))
        sc_mm, sc_max, sc_exp, pt_mm, pt_copied, pv_mm, o_copied = map(sem, (
            "sc_mm", "sc_max", "sc_exp", "pt_mm", "pt_copied", "pv_mm", "o_copied"))
        side_mm, side_copied = sem("side_mm"), sem("side_copied")
        mix_mm = [sem(f"mix_mm{n}") for n in range(3)]
        x_new = [sem(f"x_new{n}") for n in range(3)]
        sq_ready, st_mm, ms_ready, std_ready, xr_ready, h_new, h_ctx = map(sem, (
            "sq_ready", "st_mm", "ms_ready", "std_ready", "xr_ready", "h_new", "h_ctx"))
        pad_zero, diff_ready, diff2_ready, sums2_order = map(sem, ("pad_zero", "diff_ready", "diff2_ready", "sums2_order"))

        lgT_mm, lgT_copied = sem("lgT_mm"), sem("lgT_copied")
        lg_mm, lg_read, gexp, apart, texp, picked = map(sem, ("lg_mm", "lg_read", "gexp", "apart", "texp", "picked"))
        cnt_mm, over_ready, over_mm, slots_ready = map(sem, ("cnt_mm", "over_ready", "over_mm", "slots_ready"))
        hb_mm, hb_copied, s_rowsout, tab_mm, idx_ready, xg_clear = map(sem, (
            "hb_mm", "hb_copied", "s_rowsout", "tab_mm", "idx_ready", "xg_clear"))
        s_w = [sem(f"s_w{b}") for b in range(RING)]
        s_more = sem("s_more")
        LAST = [NE - RING + (b + 1) % RING for b in range(RING)]
        PER_LAYER = [2 + (LAST[b] - RING - 1 - b) // RING for b in range(RING)]
        s_xg = [sem(f"s_xg{b}") for b in range(NBUF)]
        s_y = [sem(f"s_y{b}") for b in range(NBUF)]
        xs_w, xs_g, xs_y, x_idx, x_rows, x_rowsT, x_gu, x_silu, x_hid, x_hidmm, x_hidT, x_down, x_y = (
            [sem(f"{n}{l}") for l in range(2)] for n in (
                "xs_w", "xs_g", "xs_y", "x_idx", "x_rows", "x_rowsT", "x_gu", "x_silu", "x_hid", "x_hidmm", "x_hidT",
                "x_down", "x_y"))

        def pool_group(eng, E, g, sums, order, done):
            eng.wait_ge(h_new, KD + 2 * (g + 1))
            eng.wait_ge(h_ctx, KD + 2 * (g + 1))
            eng.wait_ge(s_pool, 32)
            src, n, step = padded[:, 2 * g:2 * g + 2], PADW, 1
            while step < WINDOWS[g]:
                dst = sums[:, step.bit_length() % 2]
                n -= step
                order(E.tensor_tensor(dst[:, :, 0:n], src[:, :, 0:n], src[:, :, step:step + n], ALU.add))
                src, step = dst, 2 * step
            for first, at, m in SEGS:
                out = hT[:, 2 * g:2 * g + 2, first:first + m]
                a = at - WINDOWS[g] // 2
                order(E.tensor_tensor(out, src[:, :, a:a + m],
                                      rcount[:, g, first:first + m].unsqueeze(1).to_broadcast([P, 2, m]), ALU.mult))
                last = E.tensor_tensor(out, out, padded[:, 2 * g:2 * g + 2, at:at + m], ALU.subtract)
                if first == 0:
                    order(last)
            last.then_inc(done, 1)

        def extra_tiles(eng, n_extra, body):
            with eng.If(n_extra > 0):
                body(0)
                with eng.If(n_extra > 1):
                    with eng.Fori(1, EXTRA) as j:
                        with eng.If(n_extra > j):
                            body(j)

        def users(l, b, n):
            return l * ((NE - b + n - 1) // n)

        xg_mm, xgT_ready, gu_mm, silu_ready, hid_ready, hid_mm, hidT_ready, down_mm, y_ready = map(sem, (
            "xg_mm", "xgT_ready", "gu_mm", "silu_ready", "hid_ready", "hid_mm", "hidT_ready", "down_mm", "y_ready"))
        s_yrow, diag_ready = [sem(f"s_yrow{t}") for t in range(TT)], sem("diag_ready")
        results_in, fin_last = sem("results_in"), sem("fin_last")
        y_scaled, y_gated = sem("y_scaled"), sem("y_gated")
        x1_mm, x1_copied, g2_mm, g2_ready, fin_ready = map(sem, ("x1_mm", "x1_copied", "g2_mm", "g2_ready", "fin_ready"))

        AFTER_QKV = {g: 3 + g for g in range(1, 9)}
        FIRST_SIDE = AFTER_QKV[8] + 1
        LATE = 2 * NCH - 6
        NO_VEC = 2 * NCH - 2
        SIDE = {step: ("ada", FIRST_SIDE + i) for i, step in enumerate((1, 6, 11, 15, 26, 30))}
        SIDE.update({17: ("q", 0), 18: ("q", 1), 20: ("k", 0), 23: ("o", 1, 0), 24: ("o", 1, 1),
                     35: ("o", 2, 0), 36: ("o", 2, 1)})
        SIDE_STEPS = sorted(SIDE)
        MODS_STEP = 36
        WO_STEPS = {38 + d: d for d in range(KD)}
        ITEMS = [(t, h) for t in (1, 2, 0) for h in range(HEADS)]
        QTILES = (1, 2, 0)
        TURNED = (("q", 1, 0), ("q", 1, 1), ("k", 1, 0), ("k", 0, 0), ("k", 2, 0), ("q", 2, 0), ("q", 2, 1))
        TURNED_BANKS = (3, 4, 5, 6, 5, 3, 4)

        SCORE_BANKS = (1, 3, 4)
        POOL_ORDER = (0, 1, 4, 5, 2, 3, 6, 7)
        POOL_BANKS = (4, 5, 0, 1, 2, 3, 7, 4)

        def ada_bank(i):
            return bank[0 if FIRST_SIDE <= i < LATE else i % 2]

        def mod(l, i, k, cond):
            return mods[:, l, i * KD + k, cond:cond + 1]

        block = ctx.enter_context(nc.Block())

        @block.sync
        def _(sp):
            def load_ada(i):
                if i >= 3:
                    sp.wait_ge(ada_mm, i - 2)
                l, n = i // NCH, i % NCH
                sp.dma_start(ada_place[(i + 2) % 3], ada_w[l].rearrange("(k p) n -> p k n", p=P)[:, :, n * ACH:(n + 1) * ACH])\
                  .then_inc(s_adaw[(i + 2) % 3], 16)

            def load_expert(l, e, b, arrived):
                slot = ring[:, b, :]
                for i, w in enumerate((moe_w_gate, moe_w_up)):
                    sp.dma_start(slot[:, i * KD * FE:(i + 1) * KD * FE],
                                 w[l, bass.ds(e, 1)].rearrange("o (p k) f -> (o p) (k f)", k=KD)).then_inc(arrived, 16)
                sp.dma_start(slot[:, 2 * KD * FE:].rearrange("p (j n) -> p j n", j=2),
                             moe_w_down[l, bass.ds(e, 1)].rearrange("o (j p) d -> p (o j) d", p=P)).then_inc(arrived, 16)

            load_ada(0)
            sp.dma_start(con[:, :], consts).then_inc(s_const, 16)
            for i, v in enumerate((norm_mix_g, norm_ffn_g)):
                sp.dma_start(rowsA[16 * i:16 * i + 16, :], v.rearrange("l (k p) -> (l k) p", p=P)).then_inc(s_rows, 16)
            sp.dma_start(rowsA[32:40, :], pool_scale.rearrange("l (k p) -> (l k) p", p=P)).then_inc(s_rows, 16)
            sp.dma_start(rowsA[40:48, :], c_ctx.rearrange("(k p) -> k p", p=P)).then_inc(s_rows, 16)
            sp.dma_start(rowsA[48:56, :], c.rearrange("l (k p) -> (l k) p", p=P)).then_inc(s_rows, 16)
            sp.dma_start(rowsB[:, :], ada_b.rearrange("l (k p) -> (l k) p", p=P)).then_inc(s_rows, 16)
            sp.dma_start(xtok[:, 0, :], x_prompt[0]).then_inc(s_x, 16)
            sp.dma_start(xtok[:, 1:3, :], x_sample[0].rearrange("(t p) d -> p t d", p=P)).then_inc(s_x, 16)
            for i in range(1, 4):
                load_ada(i)
            for n in range(3):
                sp.dma_start(wqkv[n], attn_w_qkv[0].rearrange("(k p) n -> p k n", p=P)[:, :, n * 512:(n + 1) * 512])\
                  .then_inc(s_wqkv[n], 16)
                if n:
                    load_ada(3 + n)
            load_ada(6)
            load_ada(7)
            sp.dma_start(wo, attn_w_o[0].rearrange("(k p) n -> p k n", p=P)).then_inc(s_wo, 16)
            for i in range(8, LATE + 3):
                load_ada(i)

            for l in range(2):
                for b in range(l, RING):
                    if l == 0:
                        if b < 2:
                            sp.wait_ge(pv_mm, len(ITEMS))
                        else:
                            sp.wait_ge(mix_mm[0], 2 * KD)
                            if b == 3:
                                for i in range(LATE + 3, 2 * NCH):
                                    load_ada(i)
                                sp.wait_ge(ada_mm, LATE + 4)
                    elif b < 3:
                        sp.wait_ge(down_mm, LAST[b] + 1)
                    else:
                        sp.wait_ge(mix_mm[1], 1)
                    load_expert(l, b, b, s_w[b])
                if l == 0:
                    sp.wait_ge(ada_mm, 2 * NCH)
                    sp.wait_ge(ada_vec, NO_VEC)
                    sp.wait_ge(xg_mm, 1)
                else:
                    sp.wait_ge(diff2_ready, 2)
                for i, w in enumerate((moe_w_gate, moe_w_up)):
                    sp.dma_start(more_gu[:, i * KD * FE:(i + 1) * KD * FE],
                                 w[l, RING].rearrange("(p k) f -> p (k f)", k=KD)).then_inc(s_more, 16)
                sp.wait_ge(hb_mm, l * 6 + 6)
                for j in range(2):
                    sp.dma_start(more_down[j], moe_w_down[l, RING, j * P:(j + 1) * P, :]).then_inc(s_more, 16)

                def load_tile(s, b, old):
                    sp.wait_ge(down_mm, s + (l * NE + 1 - old))
                    load_expert(l, s, b, s_w[b])

                for s in range(RING + 1, 2 * RING + 1):
                    load_tile(s, s - RING - 1, RING + 1)
                loops = (NE - 2 * RING - 1) // RING
                with sp.Fori(0, loops) as r:
                    for b in range(RING):
                        load_tile(r * RING + (2 * RING + 1 + b), b, RING)
                for s in range(2 * RING + 1 + RING * loops, NE):
                    load_tile(s, (s - 1) % RING, RING)
                def load_extra(j):
                    e = sp.value_load(extra_e[0:1, bass.ds(j, 1)], min_val=0, max_val=NE - 1)
                    sp.wait_ge(down_mm, l * NE + LAST[3] + 1)
                    sp.wait_ge(x_down[l], j + 1)
                    load_expert(l, e, 3, xs_w[l])

                sp.wait_ge(x_down[l], 1)
                n_extra = sp.value_load(extra_e[0:1, EXTRA:EXTRA + 1], min_val=0, max_val=EXTRA)
                with sp.If(n_extra > 0):
                    load_extra(0)
                if l == 0:
                    sp.wait_ge(down_mm, LAST[0] + 1)
                    load_expert(1, 0, 0, s_w[0])
                with sp.If(n_extra > 1):
                    with sp.Fori(1, EXTRA) as j:
                        with sp.If(n_extra > j):
                            load_extra(j)
                sp.wait_ge(results_in, l + 1)
                for t in range(TT):
                    for k in range(2):
                        sp.dma_start(yrow[:, t, k], res_dram[l][k * NTOK + t * P:k * NTOK + (t + 1) * P, :])\
                          .then_inc(s_yrow[t], 16)

        @block.gpsimd
        def _(pool):
            G = nc.gpsimd
            G.memset(condT[:, :, :], 0.0).then_inc(cond_zero, 1)
            pool.dma_start(qg[:, 0, :], attn_q_norm[0:1, :].to_broadcast([P, HD])).then_inc(s_qg, 16)
            pool.dma_start(qg[:, 1, :], attn_k_norm[0:1, :].to_broadcast([P, HD])).then_inc(s_qg, 16)
            pool.wait_ge(qkv_mm, 7)
            pool.dma_start(cache[:, 0, :], cache_k[0, 0].rearrange("t h d -> t (h d)")).then_inc(s_cache, 16)
            pool.dma_start(cache[:, 1, :], cache_v[0, 0].rearrange("t h d -> t (h d)")).then_inc(s_cache, 16)
            pool.wait_ge(qkv_mm, 8)
            G.memset(kT[HD:P, 0], 0.0).then_inc(keys_zero, 1)
            G.memset(kT[0:HD, 1], 0.0).then_inc(keys_zero, 1)
            for l in range(2):
                pool.dma_start(wr[:, l, :, 0:NG], moe_w_group[l].rearrange("(k p) g -> p k g", p=P)).then_inc(s_wr, 16)
                for g in range(NG):
                    pool.dma_start(wr[:, l, :, NG + g * EPG:NG + (g + 1) * EPG],
                                   moe_w_expert[l, g].rearrange("(k p) e -> p k e", p=P)).then_inc(s_wr, 16)
            copies = 0
            row_limit, res_limit = pool.to_reg(2 * NTOK - 1), pool.to_reg(4 * NTOK - 1)

            for l in range(2):
                if l == 0:
                    pool.wait_ge(ada_mm, 2 * NCH - 1)
                    pool.wait_ge(s_out, 32)
                else:
                    pool.wait_ge(diff_ready, 2)
                    pool.wait_ge(diff2_ready, 2)
                G.memset(xg, 0.0).then_inc(xg_clear, 1)
                pool.wait_ge(idx_ready, l * 2 + 2)
                pool.wait_ge(xg_clear, l + 1)
                pool.wait_ge(s_rowsout, l * 48 + 16 * TT)
                rows = rows_dram[l].rearrange("t (a n) -> (t a) n", a=2)
                res = res_dram[l].rearrange("t (a n) -> (t a) n", a=2)

                def gather(s, b, copied, n, arrived):
                    G.tensor_copy(gcur[:, b:b + 1], gidx[:, bass.ds(s, 1)]).then_inc(copied, 1)
                    pool.wait_ge(copied, n + 1)
                    pool.reg_alu(row_limit, row_limit, 0, ALU.max)
                    pool.indirect_dma_start(
                        xg[:, b], None, rows, bass.IndirectOffsetOnAxis(ap=gcur[:, b:b + 1], axis=0),
                        bounds_check=row_limit, oob_is_err=False).then_inc(arrived, 16)

                def scatter(s, b, copied, n, result, m, arrived):
                    G.tensor_copy(scur[:, b:b + 1], sidx[:, bass.ds(s, 1)]).then_inc(copied, 1)
                    pool.wait_ge(copied, n + 1)
                    pool.wait_ge(result, m)
                    pool.reg_alu(res_limit, res_limit, 0, ALU.max)
                    pool.indirect_dma_start(
                        res, bass.IndirectOffsetOnAxis(ap=scur[:, b:b + 1], axis=0),
                        yout[:, b], None, bounds_check=res_limit, oob_is_err=False).then_inc(arrived, 16)

                def step(s, b, n, more=True, old=True):
                    if more:
                        pool.wait_ge(xg_mm, l * NE + s + 1)
                        gather(s + NBUF, b, pool_order, n, s_xg[b])
                        n = n + 1
                    if old:
                        pool.wait_ge(s_y[b], s * 4 + (16 * users(l, b, NBUF) - 4 * b))
                    scatter(s, b, pool_order, n, y_ready, l * NE + s + 1, s_y[b])

                pool.wait_ge(x_down[l], 1)
                n_extra = pool.value_load(extra_e[0:1, EXTRA:EXTRA + 1], min_val=0, max_val=EXTRA)
                for b in range(NBUF):
                    gather(b, b, pool_order, copies + b, s_xg[b])
                if l == 0:
                    pool.wait_ge(mix_mm[0], KD + 1)
                    pool.dma_start(rcount, counts.rearrange("p (g t) -> p g t", g=4)).then_inc(s_pool, 16)
                    pool.dma_start(poolw, pool_w[0].rearrange("g (k p) n -> p g k n", p=P)).then_inc(s_pool, 16)
                copies += NBUF
                for b in range(NBUF):
                    step(b, b, copies, old=False)
                    copies += 2
                loops = NE // NBUF - 2
                with pool.Fori(0, loops) as r:
                    for b in range(NBUF):
                        step(r * NBUF + (NBUF + b), b, r * (2 * NBUF) + (copies + 2 * b))
                copies += 2 * NBUF * loops
                for s in range(NE - NBUF, NE):
                    step(s, s % NBUF, copies, more=False)
                    copies += 1
                    if s == NE - NBUF:
                        with pool.If(n_extra > 0):
                            pool.wait_ge(xg_mm, l * NE + s + 1)
                            gather(NE, 0, x_idx[l], 0, xs_g[l])
                for b in range(NBUF):
                    pool.wait_ge(s_y[b], 16 * users(l + 1, b, NBUF))

                def extra(j):
                    if not isinstance(j, int):
                        gather(j + NE, 0, x_idx[l], j * 2, xs_g[l])
                    scatter(j + NE, 0, x_idx[l], j * 2 + 1, x_y[l], j + 1, xs_y[l])
                    pool.wait_ge(xs_y[l], j * 16 + 16)
                    pool.reg_alu(res_limit, res_limit, 0, ALU.max)

                extra_tiles(pool, n_extra, extra)
                G.memset(scur[:, 0:1], 0).then_inc(results_in, 1)
                if l == 0:
                    pool.wait_ge(mix_mm[1], 6)
                    G.memset(padded, 0.0).then_inc(pad_zero, 1)
                    pool_chain = Chain(pool, sums2_order)
                    for g in (0, 1):
                        pool_group(pool, G, g, sums2, pool_chain, diff2_ready)
                else:
                    for t in range(TT - 1):
                        pool.wait_ge(y_gated, t + 1)
                        pool.wait_ge(x1_copied, 2 * t + 2)
                        G.tensor_tensor(xtok[:, t, :], yrow[:, t, 0], xtok[:, t, :], ALU.add).then_inc(fin_ready, 1)
            pool.wait_ge(s_out, 32 + 16 * TT)

        @block.scalar
        def _(act):
            A = nc.scalar
            act.wait_ge(rows_read, 1)
            act.wait_ge(cond_zero, 1)
            for i in range(2):
                A.activation(condT[:, :, i], gains[:, 40 + 8 * i:48 + 8 * i], ACT.Silu).then_inc(cond_ready, 1)
            act.wait_ge(s_x, 32)
            for t in range(TT):
                A.activation(free[:, t * D:(t + 1) * D], xtok[:, t, :], ACT.Square,
                             accum_out=ss[:, t:t + 1]).then_inc(ss_ready, 1)
            act.wait_ge(ms_x, 1)
            A.activation(ss[:, 4:7], ss[:, 8:11], ACT.Sqrt).then_inc(std_x, 1)

            def ada_copy(i):
                act.wait_ge(ada_mm, i + 1)
                if i >= 4:
                    act.wait_ge(ada_vec, i - 3)
                A.activation(adas[:, i % 4, :], ada_bank(i)[:, :], ACT.Copy).then_inc(ada_copied, 1)

            ada_copy(0)
            for n in range(6):
                act.wait_ge(xt_mm, n + 1)
                t, q = n // 2, n % 2
                A.activation(xT[:, 4 * q:4 * q + 4, t * P:(t + 1) * P],
                             bank[4 + n % 2][:, :].rearrange("p (k t) -> p k t", k=4), ACT.Copy).then_inc(xt_copied, 1)
            for i in range(1, 4):
                ada_copy(i)
            for g in range(9):
                t, n = QTILES[g // 3], g % 3
                act.wait_ge(qkv_mm, g + 1)
                b = bank[5 + g % 3]
                A.activation(qkv[:, t, n * 512:(n + 1) * 512], b[:, :], ACT.Copy).then_inc(qkv_copied, 1)
                w = min(512, NORMED - n * 512)
                if g >= 3:
                    act.wait_ge(qk_summed, g // 3)
                else:
                    act.wait_ge(hn_mm, 6)
                A.activation(tmp[0][:, n * 512:n * 512 + w], b[:, 0:w], ACT.Square).then_inc(qkv_sq, 1)
                if g == 8:
                    act.wait_ge(keys_zero, 2)
                    n_k = 0
                    for (kind, kt, _), b in zip(TURNED, TURNED_BANKS):
                        if kind == "k":
                            n_k += 1
                            act.wait_ge(k_mm, n_k)
                            four = bank[b][:, 0:2 * P].rearrange("p (k t) -> p k t", k=2)
                            for (parity, kv) in ((0, 0), (1, 0), (0, 1), (1, 1)):
                                last = A.activation(kT[64 * parity:64 * parity + 64, parity, kv::2, (kt + 1) * P:(kt + 2) * P],
                                                    four[64 * kv:64 * kv + 64], ACT.Copy)
                            last.then_inc(k_copied, 1)
                if g:
                    ada_copy(AFTER_QKV[g])
                if n == 2:
                    act.wait_ge(qk_ms, g // 3 + 1)
                    A.activation(ss[:, 40:60], ss[:, 20:40], ACT.Sqrt).then_inc(qk_std, 1)
            sides = 0
            for i, (t, h) in enumerate(ITEMS):
                nk = P if t == 0 else 3 * P
                act.wait_ge(sc_max, i + 1)
                if i >= 3:
                    act.wait_ge(pt_mm, i - 2)
                A.activation(probs[:, i % 3, 0:nk], bank[SCORE_BANKS[i % 3]][:, 0:nk], ACT.Exp,
                             bias=ss[:, 60 + i % 3:61 + i % 3], accum_out=rt[:, i:i + 1]).then_inc(sc_exp, 1)
                if i == 15:
                    act.wait_ge(qkv_done, 3)
                    act.dma_start(new_k[0, 0].rearrange("t h d -> t (h d)"), qkv[:, 0, HEADS * HD:NORMED]).then_inc(s_out, 16)
                    act.dma_start(new_v[0, 0].rearrange("t h d -> t (h d)"), qkv[:, 0, NORMED:QKV]).then_inc(s_out, 16)
                if i in SIDE:
                    job = SIDE[i]
                    if job[0] == "ada":
                        ada_copy(job[1])
                    else:
                        sides += 1
                        act.wait_ge(side_mm, sides)
                        four = bank[0][:, :].rearrange("p (k t) -> p k t", k=4)
                        if job[0] == "q":
                            A.activation(qT[:, 4 * job[1]:4 * job[1] + 4, 0:P], four, ACT.Copy).then_inc(side_copied, 1)
                        elif job[0] == "o":
                            A.activation(hT[:, 4 * job[2]:4 * job[2] + 4, job[1] * P:(job[1] + 1) * P], four, ACT.Copy)\
                                .then_inc(side_copied, 1)
                        else:
                            for (parity, kv) in ((0, 0), (1, 0), (0, 1), (1, 1)):
                                last = A.activation(kT[64 * parity:64 * parity + 64, parity, kv::2, 0:P],
                                                    four[64 * kv:64 * kv + 64, 0:2], ACT.Copy)
                            last.then_inc(side_copied, 1)
            for n in range(2):
                act.wait_ge(side_mm, sides + n + 1)
                A.activation(hT[:, 4 * n:4 * n + 4, 0:P], bank[3 + n][:, :].rearrange("p (k t) -> p k t", k=4), ACT.Copy)\
                    .then_inc(side_copied, 1)

            def norm_act(n):
                for i in range(KD):
                    k = POOL_ORDER[i] if n == 2 else i
                    act.wait_ge(x_new[n], (KD + k + 1, 20 + 4 * (k // 4), 2 * (i + 1))[n])
                    if i >= 2:
                        act.wait_ge(st_mm, n * KD + i - 1)
                    A.activation(sq[:, i % 2], xT[:, k, :], ACT.Square).then_inc(sq_ready, 1)
                act.wait_ge(ms_ready, n + 1)
                A.activation(rstd, rstd, ACT.Sqrt).then_inc(std_ready, 1)

            def modulate_act(n, l, scale, shift, place):
                for k in range(KD):
                    act.wait_ge(xr_ready, n * KD + k + 1)
                    A.activation(place(k), hT[:, k, CTX:NTOK], ACT.Identity, bias=mod(l, shift, k, 1),
                                 scale=mod(l, scale, k, 1)).then_inc(h_new, 1)

            for l in range(2):
                if l:
                    norm_act(1)
                    act.wait_ge(pad_zero, 1)
                    modulate_act(1, 1, 1, 0, lambda k: padded[:, k, SEGS[1][1]:SEGS[1][1] + NTOK - CTX])
                norm_act(2 * l)
                if l == 0:
                    ada_copy(LATE)
                modulate_act(2 * l, l, 4, 3, lambda k: hT[:, k, CTX:NTOK])
                if l == 0:
                    ada_copy(LATE + 1)
                act.wait_ge(lgT_mm, l + 1)
                A.activation(rt[0:NG + NE, 160:160 + NTOK], bank[7][0:NG + NE, 0:NTOK], ACT.Copy).then_inc(lgT_copied, 1)
                if l == 0:
                    ada_copy(LATE + 2)
                for n in range(6):
                    t, q = n // 2, n % 2
                    act.wait_ge(hb_mm, l * 6 + n + 1)
                    A.activation(xtok[:, t, :].rearrange("p (k q) -> p q k", k=KD)[:, 64 * q:64 * q + 64, :],
                                 bank[4 + n % 2][:, :].rearrange("p (q k) -> p q k", k=KD), ACT.Copy)\
                        .then_inc(hb_copied, 1)
                    if q:
                        act.wait_ge(hb_copied, l * 6 + n + 1)
                        act.dma_start(rows_dram[l][t * P:(t + 1) * P, :], xtok[:, t, :]).then_inc(s_rowsout, 16)
                act.wait_ge(lg_read, l + 1)
                A.activation(rt[:, 112:124], rt[:, 112:124], ACT.Exp).then_inc(gexp, 1)
                act.wait_ge(apart, l + 1)
                A.activation(rt[:, 136:139], rt[:, 136:139], ACT.Exp).then_inc(texp, 1)
                if l == 0:
                    for i in range(LATE + 3, 2 * NCH):
                        ada_copy(i)
                if l == 1:
                    act.wait_ge(mix_mm[2], KD)
                    act.dma_start(bias2, ada_b[1:2, 5 * D:6 * D].to_broadcast([P, D])).then_inc(s_bias2, 16)
                    act.wait_ge(s_rowsout, 48 + 16 * TT)
                    for n in range(6):
                        t, q = n // 2, n % 2
                        act.wait_ge(x1_mm, n + 1)
                        A.activation(xtok[:, t, q * 512:(q + 1) * 512], bank[4 + n % 2][:, :], ACT.Copy)\
                            .then_inc(x1_copied, 1)

                def silu(s, p, old=True):
                    act.wait_ge(gu_mm, l * NE + s + 1)
                    if old:
                        act.wait_ge(hid_ready, l * NE + s - 1)
                    A.activation(gated[:, p], bank[p][:, 0:P], ACT.Silu).then_inc(silu_ready, 1)

                def results(s, q, old=True):
                    act.wait_ge(down_mm, l * NE + s + 1)
                    if old:
                        act.wait_ge(s_y[q], s * 4 + (16 * users(l, q, NBUF) - 4 * q))
                    A.activation(yout[:, q], bank[4 + q % 2][:, :], ACT.Copy).then_inc(y_ready, 1)

                silu(0, 0, old=False)
                for s in range(1, NBUF + 1):
                    silu(s, s % 2, old=s > 1)
                    results(s - 1, s - 1, old=False)
                loops = (NE - NBUF - 1) // NBUF
                with act.Fori(0, loops) as r:
                    for b in range(NBUF):
                        silu(r * NBUF + (NBUF + 1 + b), (1 + b) % 2)
                        results(r * NBUF + (NBUF + b), b)
                for s in range(NBUF + 1 + NBUF * loops, NE):
                    silu(s, s % 2)
                    results(s - 1, (s - 1) % NBUF)
                results(NE - 1, (NE - 1) % NBUF)
                act.wait_ge(x_down[l], 1)
                n_extra = act.value_load(extra_e[0:1, EXTRA:EXTRA + 1], min_val=0, max_val=EXTRA)

                def extra(j):
                    act.wait_ge(x_gu[l], j + 1)
                    A.activation(gated[:, 0], bank[0][:, 0:P], ACT.Silu).then_inc(x_silu[l], 1)
                    act.wait_ge(x_down[l], j + 2)
                    act.wait_ge(s_y[0], 16 * users(l + 1, 0, NBUF))
                    A.activation(yout[:, 0], bank[4][:, :], ACT.Copy).then_inc(x_y[l], 1)

                extra_tiles(act, n_extra, extra)
            for t in range(TT):
                act.wait_ge(s_yrow[t], 64)
                A.activation(yrow[:, t, 0], yrow[:, t, 0], ACT.Copy, scale=wts[:, 0, t:t + 1]).then_inc(y_scaled, 1)
            for t in range(TT):
                if t < TT - 1:
                    act.wait_ge(fin_ready, t + 1)
                else:
                    act.wait_ge(fin_last, 1)
                act.dma_start(y_prompt[0] if t == 0 else y_sample[0, (t - 1) * P:t * P, :], xtok[:, t, :]).then_inc(s_out, 16)
            act.wait_ge(s_out, 32 + 16 * TT)

        @block.vector
        def _(dve):
            V = nc.vector
            order = Chain(dve, dve_order)
            dve.wait_ge(rows_mm, 1)
            V.tensor_copy(gains[:, :], bank[3][:, 0:56]).then_inc(rows_read, 1)
            V.tensor_copy(bias[:, :, :].rearrange("p l m -> p (l m)"), bank[3][:, 64:160]).then_inc(rows_read, 1)
            dve.wait_ge(rows_read, 2)
            dve.wait_ge(ss_ready, TT)
            V.tensor_scalar(ss[:, 8:11], ss[:, 0:3], 1.0 / D, EPS, ALU.mult, ALU.add).then_inc(ms_x, 1)
            dve.wait_ge(std_x, 1)
            order(V.reciprocal(ss[:, 12:15], ss[:, 4:7]))
            dve.wait_ge(xt_mm, 6)
            for t in range(TT):
                V.tensor_scalar(xtok[:, t, :], xtok[:, t, :], ss[:, 12 + t:13 + t], None, ALU.mult).then_inc(xn_ready, 1)
            for n in range(6):
                dve.wait_ge(hn_mm, n + 1)
                t, q = n // 2, n % 2
                V.tensor_copy(hT[:, 4 * q:4 * q + 4, t * P:(t + 1) * P],
                              bank[6 + n % 2][:, :].rearrange("p (k t) -> p k t", k=4)).then_inc(hn_copied, 1)

            def modulation(l, a, b):
                cols = bank[2][:, l * 2 * NMOD + 2 * a * KD:l * 2 * NMOD + 2 * b * KD].rearrange("p (m c) -> p m c", c=2)
                m = mods[:, l, a * KD:b * KD, :]
                order(V.tensor_tensor(m, cols, bias[:, l, a * KD:b * KD].unsqueeze(2).to_broadcast([P, (b - a) * KD, 2]),
                                      ALU.add))
                for i, first in ((1, 8 * l), (4, 16 + 8 * l)):
                    if a <= i < b:
                        m = mods[:, l, i * KD:(i + 1) * KD, :]
                        order(V.tensor_scalar(m, m, 1.0, None, ALU.add))
                        order(V.tensor_tensor(m, m, gains[:, first:first + KD].unsqueeze(2).to_broadcast([P, KD, 2]),
                                              ALU.mult))

            dve.wait_ge(ada_vec, 4)
            modulation(0, 0, 2)
            V.memset(ss[:, 15:16], 0.0).then_inc(mods_ready, 1)
            dve.wait_ge(hn_copied, 6)
            for cond, a, b in reversed(CONDS):
                for k in range(KD):
                    V.tensor_scalar(hT[:, k, a:b], hT[:, k, a:b], mod(0, 1, k, cond), mod(0, 0, k, cond),
                                    ALU.mult, ALU.add).then_inc(h_ready, 1)
            dve.wait_ge(s_qg, 32)
            dve.wait_ge(s_const, 16)
            order(V.tensor_scalar(qg[:, 0, :], qg[:, 0, :], SCALE, None, ALU.mult))

            def qk_stats(g):
                dve.wait_ge(qkv_sq, 3 * g + 3)
                V.tensor_reduce(ss[:, 20:40], tmp[0].rearrange("p (h d) -> p h d", d=HD), AX.X, ALU.add)\
                    .then_inc(qk_summed, 1)
                dve.wait_ge(qk_summed, g + 1)
                V.tensor_scalar(ss[:, 20:40], ss[:, 20:40], 1.0 / HD, EPS, ALU.mult, ALU.add).then_inc(qk_ms, 1)

            def qk_norm(g):
                t = QTILES[g]
                dve.wait_ge(qk_std, g + 1)
                order(V.reciprocal(ss[:, 20:40], ss[:, 40:60]))
                qk = qkv[:, t, 0:NORMED].rearrange("p (h d) -> p h d", d=HD)
                dve.wait_ge(qkv_copied, 3 * g + 3)
                order(V.tensor_tensor(qk, qk, ss[:, 20:40].unsqueeze(2).to_broadcast([P, 20, HD]), ALU.mult))
                for i, a, b in ((0, 0, HEADS), (1, HEADS, HEADS + KVH)):
                    last = V.tensor_tensor(qk[:, a:b], qk[:, a:b], qg[:, i, :].unsqueeze(1).to_broadcast([P, b - a, HD]),
                                           ALU.mult)
                    if i == 0 or t:
                        order(last)
                if t:
                    cos = C("cos")[:, (t - 1) * HD:t * HD].unsqueeze(1).to_broadcast([P, 20, HD])
                    sin = C("sin")[:, (t - 1) * HD:t * HD]
                    for a in range(4):
                        src = a ^ 1
                        order(V.tensor_tensor(
                            tmp[1].rearrange("p (h a d) -> p h a d", a=4, d=HD // 4)[:, :, a],
                            qkv[:, t, 0:NORMED].rearrange("p (h a d) -> p h a d", a=4, d=HD // 4)[:, :, src],
                            sin[:, a * 16:(a + 1) * 16].unsqueeze(1).to_broadcast([P, 20, HD // 4]), ALU.mult))
                    order(V.tensor_tensor(qk, qk, cos, ALU.mult))
                    last = V.tensor_tensor(qk, qk, tmp[1].rearrange("p (h d) -> p h d", d=HD), ALU.add)
                last.then_inc(qkv_done, 1)

            for g in range(2):
                qk_stats(g)
                qk_norm(g)
            n = 0
            for (kind, t, q), b in zip(TURNED, TURNED_BANKS):
                if kind == "q":
                    n += 1
                    dve.wait_ge(qk_mm, n)
                    V.tensor_copy(qT[:, 4 * q:4 * q + 4, t * P:(t + 1) * P],
                                  bank[b][:, :].rearrange("p (k t) -> p k t", k=4)).then_inc(qk_copied, 1)
            qk_stats(2)
            for i in range(len(ITEMS) + 3):
                if i < len(ITEMS):
                    t, h = ITEMS[i]
                    nk = P if t == 0 else 3 * P
                    dve.wait_ge(sc_mm, i + 1)
                    if i >= 3:
                        dve.wait_ge(sc_exp, i - 2)
                    V.tensor_reduce(ss[:, 60 + i % 3:61 + i % 3], bank[SCORE_BANKS[i % 3]][:, 0:nk], AX.X, ALU.max,
                                    negate=True).then_inc(sc_max, 1)
                if i == 8:
                    qk_norm(2)
                if i == MODS_STEP:
                    dve.wait_ge(ada_vec, LATE)
                    modulation(0, 2, 6)
                    V.memset(ss[:, 16:17], 0.0).then_inc(mods_ready, 1)
                    modulation(1, 0, 3)
                    V.memset(ss[:, 17:18], 0.0).then_inc(mods_ready, 1)
                if i >= 2 and i - 2 < len(ITEMS):
                    j = i - 2
                    nk = P if ITEMS[j][0] == 0 else 3 * P
                    dve.wait_ge(pt_mm, j + 1)
                    if j >= 2:
                        dve.wait_ge(pv_mm, j - 1)
                    V.tensor_copy(probsT[:, j % 2, 0:nk], bank[5 + j % 2][:, 0:nk]).then_inc(pt_copied, 1)
                if i >= 3 and (i - 3) % 8 == 7:
                    j = i - 3
                    t, h = ITEMS[j]
                    dve.wait_ge(pv_mm, j + 1)
                    order(V.reciprocal(rt[:, 64:72], rt[:, j - 7:j + 1]))
                    V.tensor_tensor(qkv[:, t, (h - 7) * HD:(h + 1) * HD].rearrange("p (h d) -> p h d", d=HD),
                                    bank[7][:, :].rearrange("p (h d) -> p h d", d=HD),
                                    rt[:, 64:72].unsqueeze(2).to_broadcast([P, 8, HD]), ALU.mult).then_inc(o_copied, 1)
                if i in WO_STEPS:
                    d = WO_STEPS[i]
                    dve.wait_ge(mix_mm[0], d + 1)
                    V.scalar_tensor_tensor(xT[:, d, CTX:NTOK], bank[2 * (d % 2)][:, 0:NTOK - CTX], mod(0, 2, d, 1),
                                           xT[:, d, CTX:NTOK], ALU.mult, ALU.add).then_inc(x_new[0], 1)
            for d in range(KD):
                dve.wait_ge(mix_mm[0], KD + d + 1)
                V.scalar_tensor_tensor(xT[:, d, 0:CTX], bank[3 + d % 2][:, 0:CTX], mod(0, 2, d, 0),
                                       xT[:, d, 0:CTX], ALU.mult, ALU.add).then_inc(x_new[0], 1)
            m = mods[:, 1, 2 * KD:3 * KD, :]
            order(V.tensor_tensor(m, m, gains[:, 32:40].unsqueeze(2).to_broadcast([P, KD, 2]), ALU.mult))

            def add_pooled():
                for i, k in enumerate(POOL_ORDER):
                    dve.wait_ge(mix_mm[2], i + 1)
                    for cond, a, b in CONDS:
                        V.scalar_tensor_tensor(xT[:, k, a:b], bank[POOL_BANKS[i]][:, a:b], mod(1, 2, k, cond),
                                               xT[:, k, a:b], ALU.mult, ALU.add).then_inc(x_new[2], 1)

            def norm_dve(n, l, scale, shift, place):
                dve.wait_ge(st_mm, n * KD + KD)
                V.tensor_scalar(rstd, bank[6][:, 0:NTOK], 1.0 / D, EPS, ALU.mult, ALU.add).then_inc(ms_ready, 1)
                dve.wait_ge(std_ready, n + 1)
                order(V.reciprocal(rstd, rstd))
                V.tensor_tensor(hT[:, 0, :], xT[:, 0, :], rstd, ALU.mult).then_inc(xr_ready, 1)
                for k in range(KD):
                    if k + 1 < KD:
                        V.tensor_tensor(hT[:, k + 1, :], xT[:, k + 1, :], rstd, ALU.mult).then_inc(xr_ready, 1)
                    dve.wait_ge(xr_ready, n * KD + k + 1)
                    V.tensor_scalar(place(k), hT[:, k, 0:CTX], mod(l, scale, k, 0), mod(l, shift, k, 0),
                                    ALU.mult, ALU.add).then_inc(h_ctx, 1)

            def pick(values, mark, rev, best, n):
                shape = [P, TT, n]
                order(V.tensor_reduce(best, values, AX.X, ALU.max))
                order(V.tensor_tensor(mark, values, best.unsqueeze(2).to_broadcast(shape), ALU.is_equal))
                order(V.tensor_tensor(mark, mark, rev.unsqueeze(1).to_broadcast(shape), ALU.mult))
                order(V.tensor_reduce(rt[:, 108:111], mark, AX.X, ALU.max))
                order(V.tensor_tensor(mark, mark, rt[:, 108:111].unsqueeze(2).to_broadcast(shape), ALU.is_equal))

            def router(l):
                lg = rt[:, 0:108].rearrange("p (t e) -> p t e", t=TT)
                e32 = [rt[:, 160 + 96 * i:256 + 96 * i].rearrange("p (t e) -> p t e", t=TT) for i in range(5)]
                masked, first, second, both, work = e32
                gbest, m1, m2 = rt[:, 140:143], rt[:, 144:147], rt[:, 148:151]
                ge, gmark, far = rt[:, 112:124], rt[:, 124:136].rearrange("p (t g) -> p t g", t=TT), rt[:, 136:139]
                dve.wait_ge(lg_mm, l + 1)
                order(V.tensor_copy(rt[:, 0:108], bank[7][:, 0:108]))
                pick(lg[:, :, 0:NG], gmark, C("revg"), gbest, NG)
                V.tensor_tensor(ge.rearrange("p (t g) -> p t g", t=TT), lg[:, :, 0:NG],
                                gbest.unsqueeze(2).to_broadcast([P, TT, NG]), ALU.subtract).then_inc(lg_read, 1)
                m4 = masked.rearrange("p t (g e) -> p t g e", g=NG)
                for t in range(TT):
                    order(V.tensor_tensor(m4[:, t], lg[:, t, NG:].rearrange("p (g e) -> p g e", g=NG),
                                          gmark[:, t].unsqueeze(2).to_broadcast([P, NG, EPG]), ALU.mult))
                order(V.tensor_scalar(gmark, gmark, 1e30, -1e30, ALU.mult, ALU.add))
                for t in range(TT):
                    order(V.tensor_tensor(m4[:, t], m4[:, t], gmark[:, t].unsqueeze(2).to_broadcast([P, NG, EPG]), ALU.add))
                pick(masked, first, C("rev"), m1, NE)
                order(V.scalar_tensor_tensor(masked, first, -2e30, masked, ALU.mult, ALU.add))
                pick(masked, second, C("rev"), m2, NE)
                V.tensor_tensor(far, m2, m1, ALU.subtract).then_inc(apart, 1)
                V.tensor_tensor(both, first, second, ALU.add).then_inc(picked, 1)
                dve.wait_ge(cnt_mm, l + 1)
                over, tile_n = rt[0:NE, 152:153], rt[0:NE, 153:154]
                order(V.tensor_copy(tile_n, bank[6][0:NE, 128:129]))
                order(V.tensor_scalar(over, tile_n, float(TC), None, ALU.is_gt))
                for j in range(2, NTOK // TC):
                    order(V.scalar_tensor_tensor(over, tile_n, float(TC * j), over, ALU.is_gt, ALU.add))
                V.tensor_scalar(work[0:NE].rearrange("p t e -> p (t e)")[:, 0:96], ones[0:NE, 0:96], over, None,
                                ALU.mult).then_inc(over_ready, 1)
                V.tensor_scalar(rt[0:NE, 48:80], ones[0:NE, 0:32], over, None, ALU.mult).then_inc(over_ready, 1)
                dve.wait_ge(hb_mm, l * 6 + 6)
                dve.wait_ge(over_mm, l + 1)
                jump = rt[:, 0:NE]
                order(V.tensor_tensor(jump, bank[7][:, 128:128 + NE], C("rev"), ALU.add))
                order(V.tensor_scalar(jump, jump, float(TC), -float(TC), ALU.mult, ALU.add))
                pos = bank[6][:, 0:96].rearrange("p (t e) -> p t e", t=TT)
                shape = [P, TT, NE]
                order(V.tensor_scalar(work, pos, float(TC), None, ALU.is_ge))
                order(V.tensor_tensor(work, work, jump.unsqueeze(1).to_broadcast(shape), ALU.mult))
                order(V.tensor_tensor(work, work, C("first").unsqueeze(1).to_broadcast(shape), ALU.add))
                order(V.tensor_tensor(work, work, pos, ALU.add))
                for k, mark in enumerate((first, second)):
                    order(V.tensor_tensor(mark, mark, work, ALU.mult))
                    order(V.tensor_reduce(rt[:, 36 + 3 * k:39 + 3 * k], mark, AX.X, ALU.add))
                tile_at, place_at = rt[:, 42:48], rt[:, 96:102]
                by_tile = [P, 6, NT]
                order(V.tensor_tensor(in_tile, rt[:, 36:42].unsqueeze(2).to_broadcast(by_tile),
                                      C("tiles").unsqueeze(1).to_broadcast(by_tile), ALU.is_ge))
                order(V.tensor_reduce(tile_at, in_tile, AX.X, ALU.add))
                order(V.tensor_scalar(tile_at, tile_at, float(TC), -float(TC), ALU.mult, ALU.add))
                order(V.tensor_tensor(place_at, rt[:, 36:42], tile_at, ALU.subtract))
                V.tensor_tensor(in_tile, C("tiles").unsqueeze(1).to_broadcast(by_tile),
                                tile_at.unsqueeze(2).to_broadcast(by_tile), ALU.is_equal)
                for i in range(6):
                    V.tensor_scalar(at_place[:, i], C("place"), place_at[:, i:i + 1], C("assign")[:, i:i + 1],
                                    ALU.is_equal, ALU.mult).then_inc(slots_ready, 1)
                count = rt[0:1, 160:160 + EXTRA * NE].rearrange("p (j e) -> p j e", j=EXTRA)
                order(V.tensor_copy(rt[0:1, 48:80], bank[7][0:1, 160:192]))
                order(V.tensor_tensor(count, rt[0:1, 48:80].unsqueeze(1).to_broadcast([1, EXTRA, NE]),
                                      C("extra")[0:1].unsqueeze(2).to_broadcast([1, EXTRA, NE]), ALU.is_le))
                order(V.tensor_reduce(rt[0:1, 80:80 + EXTRA], count, AX.X, ALU.add))
                order(V.tensor_scalar(rt[0:1, 80:80 + EXTRA], rt[0:1, 80:80 + EXTRA], float(NE - 1), None, ALU.min))
                order(V.tensor_copy(rt[0:1, 80 + EXTRA:81 + EXTRA], rt[0:1, 79:80]))
                V.tensor_copy(extra_e[0:1, :], rt[0:1, 80:81 + EXTRA]).then_inc(x_down[l], 1)
                dve.wait_ge(gexp, l + 1)
                dve.wait_ge(apart, l + 1)
                order(V.tensor_reduce(gbest, ge.rearrange("p (t g) -> p t g", t=TT), AX.X, ALU.add))
                dve.wait_ge(texp, l + 1)
                order(V.tensor_scalar(m1, far, 1.0, None, ALU.add))
                order(V.tensor_tensor(m1, m1, gbest, ALU.mult))
                order(V.reciprocal(wts[:, 0, :], m1))
                order(V.tensor_tensor(wts[:, 1, :], wts[:, 0, :], far, ALU.mult))
                dve.wait_ge(tab_mm, l + 1)
                name, at = bank[3][:, 0:NT], rt[:, 256:256 + NT]
                order(V.tensor_scalar(at, name, NTOK - NONE, -float(NTOK), ALU.is_ge, ALU.mult))
                order(V.tensor_tensor(at, at, name, ALU.add))
                V.tensor_scalar(gidx[:, :], at, 2.0, C("half"), ALU.mult, ALU.add).then_inc(idx_ready, 1)
                V.tensor_scalar(sidx[:, :], name, 2.0, C("half"), ALU.mult, ALU.add).then_inc(idx_ready, 1)
                if l == 0:
                    dve.wait_ge(ada_vec, NO_VEC)
                    modulation(1, 3, 5)
                    V.memset(ss[:, 18:19], 0.0).then_inc(mods_ready, 1)
                    for t in range(TT):
                        for k in range(2):
                            V.tensor_scalar(diag[:, 2 * t + k], ident, wts[:, k, t:t + 1], None, ALU.mult)\
                                .then_inc(diag_ready, 1)

            def experts(l):
                def rows_T(s, p, old=True):
                    dve.wait_ge(xg_mm, l * NE + s + 1)
                    if old:
                        dve.wait_ge(gu_mm, l * NE + s - 1)
                    V.tensor_copy(xgT[:, p], bank[2][:, :]).then_inc(xgT_ready, 1)

                def hidden(s, p, old=True):
                    dve.wait_ge(silu_ready, l * NE + s + 1)
                    if old:
                        dve.wait_ge(hid_mm, l * NE + s - 1)
                    V.tensor_tensor(hid[:, p], bank[p][:, P:2 * P], gated[:, p], ALU.mult).then_inc(hid_ready, 1)

                def hidden_T(s, p, old=True):
                    dve.wait_ge(hid_mm, l * NE + s + 1)
                    if old:
                        dve.wait_ge(down_mm, l * NE + s - 1)
                    V.tensor_copy(hidT[:, p], bank[3][:, 0:P]).then_inc(hidT_ready, 1)

                rows_T(0, 0, old=False)
                rows_T(1, 1, old=False)
                hidden(0, 0, old=False)
                hidden_T(0, 0, old=False)
                rows_T(2, 0)
                hidden(1, 1, old=False)
                hidden_T(1, 1, old=False)
                loops = (NE - 3) // 2
                with dve.Fori(0, loops) as r:
                    for b in range(2):
                        rows_T(r * 2 + (3 + b), 1 - b)
                        hidden(r * 2 + (2 + b), b)
                        hidden_T(r * 2 + (2 + b), b)
                for s in range(2 + 2 * loops, NE):
                    if s + 1 < NE:
                        rows_T(s + 1, (s + 1) % 2)
                    hidden(s, s % 2)
                    hidden_T(s, s % 2)
                n_extra = dve.value_load(extra_e[0:1, EXTRA:EXTRA + 1], min_val=0, max_val=EXTRA)

                def extra(j):
                    dve.wait_ge(x_rows[l], j + 1)
                    V.tensor_copy(xgT[:, 0], bank[2][:, :]).then_inc(x_rowsT[l], 1)
                    dve.wait_ge(x_silu[l], j + 1)
                    V.tensor_tensor(hid[:, 0], bank[0][:, P:2 * P], gated[:, 0], ALU.mult).then_inc(x_hid[l], 1)
                    dve.wait_ge(x_hidmm[l], j + 1)
                    V.tensor_copy(hidT[:, 0], bank[3][:, 0:P]).then_inc(x_hidT[l], 1)

                extra_tiles(dve, n_extra, extra)

            norm_dve(0, 0, 4, 3, lambda k: hT[:, k, 0:CTX])
            router(0)
            experts(0)
            for n in range(6):
                t, q = n // 2, n % 2
                dve.wait_ge(mix_mm[1], n + 1)
                for k in range(4 * q, 4 * q + 4):
                    part = xT[:, k, t * P:(t + 1) * P]
                    V.scalar_tensor_tensor(part, bank[4 + n % 2][:, (k % 4) * P:(k % 4 + 1) * P], mod(0, 5, k, int(t > 0)),
                                           part, ALU.mult, ALU.add).then_inc(x_new[1], 1)
            dve.wait_ge(pad_zero, 1)
            norm_dve(1, 1, 1, 0, lambda k: padded[:, k, SEGS[0][1]:SEGS[0][1] + CTX])
            for g in (2, 3):
                pool_group(dve, V, g, sums, order, diff_ready)
            add_pooled()
            norm_dve(2, 1, 4, 3, lambda k: hT[:, k, 0:CTX])
            router(1)
            dve.wait_ge(s_bias2, 16)
            for n in range(4):
                dve.wait_ge(g2_mm, n + 1)
                a = (n % 2) * 512
                V.tensor_tensor(gate2[:, n // 2, a:a + 512], bank[6 + n % 2][:, :], bias2[:, a:a + 512], ALU.add)\
                    .then_inc(g2_ready, 1)
            experts(1)
            dve.wait_ge(g2_ready, 4)
            for t in range(TT):
                y = yrow[:, t, 0]
                dve.wait_ge(y_scaled, t + 1)
                order(V.scalar_tensor_tensor(y, yrow[:, t, 1], wts[:, 1, t:t + 1], y, ALU.mult, ALU.add))
                V.tensor_tensor(y, y, gate2[:, 0 if t == 0 else 1], ALU.mult).then_inc(y_gated, 1)
            dve.wait_ge(y_gated, TT)
            dve.wait_ge(x1_copied, 2 * TT)
            V.tensor_tensor(xtok[:, TT - 1, :], yrow[:, TT - 1, 0], xtok[:, TT - 1, :], ALU.add).then_inc(fin_last, 1)

        @block.tensor
        def _(pe):
            T = nc.tensor
            pe.wait_ge(s_const, 16)
            pe.wait_ge(s_rows, 96)
            T.transpose(bank[3][:, 0:56], rowsA[:, :], ident[0:56, 0:56])
            T.transpose(bank[3][:, 64:160], rowsB[:, :], ident[0:96, 0:96]).then_inc(rows_mm, 1)
            def ada(i):
                if i == 0:
                    pe.wait_ge(cond_ready, 2)
                if FIRST_SIDE < i <= LATE:
                    pe.wait_ge(ada_copied, i)
                elif i >= 2:
                    pe.wait_ge(ada_copied, i - 1)
                pe.wait_ge(s_adaw[(i + 2) % 3], 16 * (i // 3 + 1))
                out = ada_bank(i)
                for half in range(2):
                    for j in range(4):
                        k = 4 * half + j
                        last = T.matmul(out[32 * j:32 * j + 32, :], condT[:, k, :], ada_place[(i + 2) % 3][:, k, :],
                                        start=half == 0, stop=half == 1, skip_group_check=True)
                last.then_inc(ada_mm, 1)

            def ada_vectors(i):
                pe.wait_ge(ada_copied, i + 1)
                l, n = i // NCH, i % NCH
                for j in range(ACH // P):
                    at = l * 2 * NMOD + 2 * (n * ACH // P + j)
                    last = T.matmul(bank[2][:, at:at + 2], adas[:, i % 4, j * P:(j + 1) * P], C("sel2"),
                                    start=True, stop=True)
                last.then_inc(ada_vec, 1)

            ada(0)
            pe.wait_ge(s_x, 32)
            for n in range(6):
                t, q = n // 2, n % 2
                if n >= 2:
                    pe.wait_ge(xt_copied, n - 1)
                for k in range(4):
                    last = T.transpose(bank[4 + n % 2][:, k * P:(k + 1) * P],
                                       xtok[:, t, (4 * q + k) * P:(4 * q + k + 1) * P], ident)
                last.then_inc(xt_mm, 1)
            for n in range(6):
                t, q = n // 2, n % 2
                pe.wait_ge(xn_ready, TT)
                if n >= 2:
                    pe.wait_ge(hn_copied, n - 1)
                for k in range(4):
                    last = T.transpose(bank[6 + n % 2][:, k * P:(k + 1) * P],
                                       xtok[:, t, (4 * q + k) * P:(4 * q + k + 1) * P], ident)
                last.then_inc(hn_mm, 1)
            for i in range(1, 4):
                ada(i)
                ada_vectors(i - 1)
            ada_vectors(3)

            def turn(n):
                (kind, t, q), b = TURNED[n], TURNED_BANKS[n]
                if n == 4:
                    pe.wait_ge(k_copied, 1)
                elif kind == "k":
                    pe.wait_ge(qkv_sq, 9)
                elif n >= 5:
                    pe.wait_ge(qk_copied, n - 4)
                if t:
                    pe.wait_ge(qkv_done, t)
                else:
                    pe.wait_ge(s_cache, 32)
                src = cache[:, 0] if t == 0 else qkv[:, t, HEADS * HD:NORMED] if kind == "k" else qkv[:, t, 512 * q:512 * q + 512]
                for k in range(4 if kind == "q" else 2):
                    last = T.transpose(bank[b][:, k * P:(k + 1) * P], src[:, k * P:(k + 1) * P], ident)
                last.then_inc(qk_mm if kind == "q" else k_mm, 1)

            pe.wait_ge(xt_copied, 6)
            for g in range(9):
                t, n = QTILES[g // 3], g % 3
                pe.wait_ge(s_wqkv[n], 16)
                if g >= 3:
                    pe.wait_ge(qkv_sq, g - 2)
                for k in range(KD):
                    if g == 0:
                        pe.wait_ge(h_ready, k + 1)
                    if g == 6:
                        pe.wait_ge(h_ready, 2 * KD)
                    last = T.matmul(bank[5 + g % 3][:, :], hT[:, k, t * P:(t + 1) * P], wqkv[n][:, k, :],
                                    start=k == 0, stop=k == KD - 1)
                last.then_inc(qkv_mm, 1)
                if g == 0:
                    pe.wait_ge(mods_ready, 1)
                if g == 8:
                    for n in range(2, len(TURNED)):
                        turn(n)
                if g:
                    ada(AFTER_QKV[g])
                if g > 1:
                    ada_vectors(AFTER_QKV[g] - 1)
                if g == 6:
                    turn(0)
                    turn(1)
            ada_vectors(AFTER_QKV[8])
            pe.wait_ge(qk_copied, 4)
            pe.wait_ge(k_copied, 3)
            pe.wait_ge(ada_copied, FIRST_SIDE)
            sides = 0
            for i in range(len(ITEMS) + 3):
                if i < len(ITEMS):
                    t, h = ITEMS[i]
                    keys = slice(0, P) if t == 0 else slice(P, KEYS)
                    if i >= 3:
                        pe.wait_ge(sc_exp, i - 2)
                    if i == 2 * HEADS:
                        pe.wait_ge(side_copied, 3)
                    T.matmul(bank[SCORE_BANKS[i % 3]][:, 0:keys.stop - keys.start], qT[:, h // 2, t * P:(t + 1) * P],
                             kT[:, h % 2, h // 4, keys], start=True, stop=True).then_inc(sc_mm, 1)
                if i >= 2 and i - 2 < len(ITEMS):
                    j = i - 2
                    nb = 1 if ITEMS[j][0] == 0 else 3
                    pe.wait_ge(sc_exp, j + 1)
                    if j >= 2:
                        pe.wait_ge(pt_copied, j - 1)
                    for k in range(nb):
                        last = T.transpose(bank[5 + j % 2][:, k * P:(k + 1) * P], probs[:, j % 3, k * P:(k + 1) * P], ident)
                    last.then_inc(pt_mm, 1)
                if i >= 3:
                    j = i - 3
                    t, h = ITEMS[j]
                    vcols = slice(NORMED + h // 4 * HD, NORMED + (h // 4 + 1) * HD)
                    values = [qkv[:, 0, vcols]] if t == 0 else [cache[:, 1, h // 4 * HD:(h // 4 + 1) * HD],
                                                                qkv[:, 1, vcols], qkv[:, 2, vcols]]
                    pe.wait_ge(pt_copied, j + 1)
                    if j % 8 == 0 and j:
                        pe.wait_ge(o_copied, j // 8)
                    for k, v in enumerate(values):
                        last = T.matmul(bank[7][:, (h % 8) * HD:(h % 8 + 1) * HD], probsT[:, j % 2, k * P:(k + 1) * P], v,
                                        start=k == 0, stop=k == len(values) - 1)
                    last.then_inc(pv_mm, 1)
                if i in SIDE:
                    job, before = SIDE[i], SIDE_STEPS.index(i)
                    before = SIDE[SIDE_STEPS[before - 1]][0] if before else "ada"
                    if job[0] == "ada":
                        if before != "ada":
                            pe.wait_ge(side_copied, sides)
                        ada(job[1])
                        if job[1] > FIRST_SIDE:
                            ada_vectors(job[1] - 1)
                    else:
                        if before == "ada":
                            done = max(SIDE[m][1] for m in SIDE_STEPS if m < i and SIDE[m][0] == "ada")
                            pe.wait_ge(ada_copied, done + 1)
                        else:
                            pe.wait_ge(side_copied, sides)
                        sides += 1
                        if job[0] == "q":
                            pe.wait_ge(qkv_done, 3)
                            src = qkv[:, 0, 512 * job[1]:512 * job[1] + 512]
                        elif job[0] == "k":
                            src = qkv[:, 0, HEADS * HD:NORMED]
                        else:
                            pe.wait_ge(o_copied, 2 * job[1])
                            src = qkv[:, job[1], 512 * job[2]:512 * job[2] + 512]
                        for k in range(src.shape[1] // P):
                            last = T.transpose(bank[0][:, k * P:(k + 1) * P], src[:, k * P:(k + 1) * P], ident)
                        last.then_inc(side_mm, 1)
                if i == 34:
                    ada_vectors(LATE - 1)
                if i in WO_STEPS:
                    d = WO_STEPS[i]
                    if d == 0:
                        pe.wait_ge(s_wo, 16)
                        pe.wait_ge(mods_ready, 3)
                        pe.wait_ge(side_copied, sides)
                    if d >= 2:
                        pe.wait_ge(x_new[0], d - 1)
                    for k in range(KD):
                        last = T.matmul(bank[2 * (d % 2)][:, 0:NTOK - CTX], wo[:, k, d * P:(d + 1) * P], hT[:, k, CTX:NTOK],
                                        start=k == 0, stop=k == KD - 1)
                    last.then_inc(mix_mm[0], 1)
            pe.wait_ge(o_copied, 6)
            for n in range(2):
                for k in range(4):
                    last = T.transpose(bank[3 + n][:, k * P:(k + 1) * P], qkv[:, 0, (4 * n + k) * P:(4 * n + k + 1) * P], ident)
                last.then_inc(side_mm, 1)
            pe.wait_ge(side_copied, sides + 2)
            for d in range(KD):
                if d >= 2:
                    pe.wait_ge(x_new[0], KD + d - 1)
                for k in range(KD):
                    last = T.matmul(bank[3 + d % 2][:, 0:CTX], wo[:, k, d * P:(d + 1) * P], hT[:, k, 0:CTX],
                                    start=k == 0, stop=k == KD - 1)
                last.then_inc(mix_mm[0], 1)

            def norm_pe(n):
                for k in range(KD):
                    pe.wait_ge(sq_ready, n * KD + k + 1)
                    T.matmul(bank[6][:, 0:NTOK], ones, sq[:, k % 2], start=k == 0, stop=k == KD - 1).then_inc(st_mm, 1)

            for l in range(2):
                norm_pe(2 * l)
                if l == 0:
                    pe.wait_ge(x_new[0], KD)
                    ada(LATE)
                    ada(LATE + 1)
                if l == 0:
                    pe.wait_ge(s_wr, 160)
                for k in range(KD):
                    pe.wait_ge(h_new, 2 * l * KD + k + 1)
                    pe.wait_ge(h_ctx, 2 * l * KD + k + 1)
                    last = T.matmul(bank[7][0:NG + NE, 0:NTOK], wr[:, l, k, :], hT[:, k, :], start=k == 0, stop=k == KD - 1)
                last.then_inc(lgT_mm, 1)
                pe.wait_ge(lgT_copied, l + 1)
                for t in range(TT):
                    last = T.transpose(bank[7][:, t * 36:(t + 1) * 36], rt[0:NG + NE, 160 + t * P:160 + (t + 1) * P],
                                       ident[0:NG + NE, 0:NG + NE])
                last.then_inc(lg_mm, 1)
                if l == 0:
                    ada_vectors(LATE)
                    ada(LATE + 2)
                    ada_vectors(LATE + 1)
                def rows_by_token(n):
                    t, q = n // 2, n % 2
                    if n >= 2:
                        pe.wait_ge(hb_copied, l * 6 + n - 1)
                    for k in range(4):
                        last = T.transpose(bank[4 + n % 2][:, k * P:(k + 1) * P], hT[:, 4 * q + k, t * P:(t + 1) * P], ident)
                    last.then_inc(hb_mm, 1)
                for n in range(6):
                    rows_by_token(n)
                pe.wait_ge(picked, l + 1)
                both = rt[:, 160 + 96 * 3:256 + 96 * 3].rearrange("p (t e) -> p t e", t=TT)
                for t in range(TT):
                    for j in range(t + 1):
                        T.matmul(bank[6][:, t * NE:(t + 1) * NE], upper if j == t else ones, both[:, j],
                                 start=j == 0, stop=j == t)
                for t in range(TT):
                    last = T.matmul(bank[6][0:NE, 128:129], both[:, t], ones[:, 0:1], start=t == 0, stop=t == TT - 1)
                last.then_inc(cnt_mm, 1)
                pe.wait_ge(over_ready, l * 2 + 2)
                parts = ((rt[0:NE, 160 + 96 * 4:256 + 96 * 4], 0, 96), (rt[0:NE, 48:80], 96, P))
                for lhs, a, b in parts:
                    T.matmul(bank[7][a:b, 128:128 + NE], lhs, upper[0:NE, 0:NE], start=True, stop=True)
                for m, sel in enumerate((upper, ident)):
                    last = T.matmul(bank[7][0:96, 160:160 + NE], parts[0][0], sel[0:NE, 0:NE], start=m == 0, stop=m == 1)
                last.then_inc(over_mm, 1)
                if l == 1:
                    pe.wait_ge(hb_copied, 6 + 6)
                    for n in range(6):
                        t, q = n // 2, n % 2
                        if n >= 2:
                            pe.wait_ge(x1_copied, n - 1)
                        for k in range(4):
                            last = T.transpose(bank[4 + n % 2][:, k * P:(k + 1) * P], xT[:, 4 * q + k, t * P:(t + 1) * P], ident)
                        last.then_inc(x1_mm, 1)
                    pe.wait_ge(x1_copied, 6)
                if l == 0:
                    for i in range(LATE + 3, 2 * NCH - 1):
                        ada(i)
                        ada_vectors(i - 1)
                pe.wait_ge(slots_ready, l * 6 + 6)
                for i in range(6):
                    last = T.matmul(bank[3][:, 0:NT], at_place[:, i], in_tile[:, i], start=i == 0, stop=i == 5)
                last.then_inc(tab_mm, 1)
                if l == 0:
                    ada(2 * NCH - 1)
                if l == 1:
                    pe.wait_ge(x_down[1], 1)
                    for n in range(4):
                        if n >= 2:
                            pe.wait_ge(g2_ready, n - 1)
                        T.matmul(bank[6 + n % 2][:, :], C("rep")[:, (n // 2) * P:(n // 2 + 1) * P],
                                 adas[:, (2 * NCH - 2 + n % 2) % 4, :], start=True, stop=True).then_inc(g2_mm, 1)
                pe.wait_ge(idx_ready, l * 2 + 2)

                def rows_T(s, q, old=True):
                    pe.wait_ge(s_xg[q], s * 4 + (16 * users(l, q, NBUF) + 16 - 4 * q))
                    if old:
                        pe.wait_ge(xgT_ready, l * NE + s)
                    rows_T_mm(q).then_inc(xg_mm, 1)

                def rows_T_mm(q):
                    for i in range(4):
                        last = T.transpose(bank[2][:, i * P:(i + 1) * P], xg[:, q, i * P:(i + 1) * P], ident)
                    return last

                def gate_up(s, p, b, old=True):
                    pe.wait_ge(xgT_ready, l * NE + s + 1)
                    if b == RING:
                        pe.wait_ge(s_more, 64 * l + 64)
                    elif isinstance(s, int) and s < RING:
                        pe.wait_ge(s_w[b], 48 * (l * PER_LAYER[b] + 1))
                    else:
                        pe.wait_ge(s_w[b], s * 12 + (48 * (l * PER_LAYER[b] + 2) - 12 * (RING + 1 + b)))
                    if old:
                        pe.wait_ge(hid_ready, l * NE + s - 1)
                    gate_up_mm(p, b).then_inc(gu_mm, 1)

                def gate_up_mm(p, b):
                    w = (more_gu if b == RING else ring[:, b, 0:2 * KD * FE]).rearrange("p (g k f) -> p g k f", g=2, k=KD)
                    xk = xgT[:, p].rearrange("p (i a c) -> p i a c", i=4, a=2)
                    for k in range(KD):
                        for a in range(2):
                            last = T.matmul(bank[p][64 * a:64 * a + 64, 0:2 * P], xk[:, k % 4, k // 4],
                                            w[:, :, k, a * P:(a + 1) * P], start=k == 0, stop=k == KD - 1,
                                            skip_group_check=True)
                    return last

                def hidden_T(s, p, old=True):
                    pe.wait_ge(hid_ready, l * NE + s + 1)
                    if old:
                        pe.wait_ge(hidT_ready, l * NE + s)
                    T.transpose(bank[3][:, 0:P], hid[:, p], ident).then_inc(hid_mm, 1)

                def down(s, p, b, old=True):
                    pe.wait_ge(hidT_ready, l * NE + s + 1)
                    if old:
                        pe.wait_ge(y_ready, l * NE + s - 1)
                    down_products(p, b).then_inc(down_mm, 1)

                def down_products(p, b):
                    w = more_down if b == RING else [ring[:, b, (2 * KD + KD // 2 * j) * FE:(2 * KD + KD // 2 * (j + 1)) * FE]
                                                     for j in range(2)]
                    for j in range(2):
                        for a in range(2):
                            last = T.matmul(bank[4 + p][64 * a:64 * a + 64, :], hidT[:, p, 64 * j:64 * j + 64],
                                            w[j][:, a * 512:(a + 1) * 512], start=j == 0, stop=j == 1,
                                            skip_group_check=True)
                    return last

                def place(s, q):
                    if isinstance(s, int) and s <= RING:
                        return s
                    return (q - 1) % RING

                def step(s, q, more=True, old=2):
                    gate_up(s, q % 2, place(s, q), old=old >= 1)
                    if more:
                        rows_T(s + 1, (q + 1) % NBUF)
                    down(s - 1, (q + 1) % 2, place(s - 1, (q - 1) % NBUF), old=old >= 2)
                    hidden_T(s, q % 2)

                if l == 0:
                    pe.wait_ge(mods_ready, 4)
                    pe.wait_ge(ada_copied, 2 * NCH - 1)
                rows_T(0, 0, old=False)
                gate_up(0, 0, 0, old=False)
                rows_T(1, 1)
                if l == 0:
                    pe.wait_ge(ada_copied, 2 * NCH)
                hidden_T(0, 0, old=False)
                first = RING + 2
                for s in range(1, first):
                    step(s, s % NBUF, old=s - 1)
                loops = (NE - 1 - first) // RING
                with pe.Fori(0, loops) as r:
                    for q in range(RING):
                        step(r * RING + (first + q), (first + q) % RING)
                for s in range(first + RING * loops, NE):
                    step(s, s % NBUF, more=s + 1 < NE)
                down(NE - 1, (NE - 1) % 2, place(NE - 1, (NE - 1) % NBUF))
                pe.wait_ge(x_down[l], 1)
                n_extra = pe.value_load(extra_e[0:1, EXTRA:EXTRA + 1], min_val=0, max_val=EXTRA)
                pe.wait_ge(y_ready, l * NE + NE)

                def extra(j):
                    pe.wait_ge(xs_g[l], j * 16 + 16)
                    rows_T_mm(0).then_inc(x_rows[l], 1)
                    pe.wait_ge(x_rowsT[l], j + 1)
                    pe.wait_ge(xs_w[l], j * 48 + 48)
                    gate_up_mm(0, 3).then_inc(x_gu[l], 1)
                    pe.wait_ge(x_hid[l], j + 1)
                    T.transpose(bank[3][:, 0:P], hid[:, 0], ident).then_inc(x_hidmm[l], 1)
                    pe.wait_ge(x_hidT[l], j + 1)
                    down_products(0, 3).then_inc(x_down[l], 1)

                extra_tiles(pe, n_extra, extra)
                if l == 0:
                    pe.wait_ge(diag_ready, 6)
                    pe.wait_ge(y_ready, NE)
                    for n in range(6):
                        t, q = n // 2, n % 2
                        pe.wait_ge(s_yrow[t], 32)
                        if n >= 2:
                            pe.wait_ge(x_new[1], 4 * (n - 1))
                        for k in range(4):
                            for c2 in range(2):
                                last = T.matmul(bank[4 + n % 2][:, k * P:(k + 1) * P],
                                                yrow[:, t, c2, (4 * q + k) * P:(4 * q + k + 1) * P], diag[:, 2 * t + c2],
                                                start=c2 == 0, stop=c2 == 1)
                        last.then_inc(mix_mm[1], 1)
                    norm_pe(1)
                    pe.wait_ge(s_pool, 32)
                    pe.wait_ge(x_new[1], 24)
                    for i, k in enumerate(POOL_ORDER):
                        g = k // 2
                        if g < 2:
                            pe.wait_ge(diff2_ready, g + 1)
                        else:
                            pe.wait_ge(diff_ready, g - 1)
                        if i == KD - 1:
                            pe.wait_ge(x_new[2], 2)
                        for j in range(2):
                            last = T.matmul(bank[POOL_BANKS[i]][:, 0:NTOK], poolw[:, g, j, (k % 2) * P:(k % 2 + 1) * P],
                                            hT[:, 2 * g + j, :], start=j == 0, stop=j == 1)
                        last.then_inc(mix_mm[2], 1)


_INS = ["x_prompt", "x_sample", "c", "cache_k", "cache_v", "c_ctx", "norm_mix_g", "norm_ffn_g", "ada_w", "ada_b",
        "attn_w_qkv", "attn_q_norm", "attn_k_norm", "attn_w_o", "pool_w", "pool_scale", "moe_w_group",
        "moe_w_expert", "moe_w_gate", "moe_w_up", "moe_w_down"]
_OUTS = [(1, CTX, D), (1, NTOK - CTX, D), (1, 1, CTX, KVH, HD), (1, 1, CTX, KVH, HD)]


def kernel(**inputs):
    import concourse.bacc as bacc
    from concourse.bass_utils import run_bass_kernel_spmd

    nc = bacc.Bacc("TRN2", target_bir_lowering=False, num_devices=1)
    arrays = {f"in_{n}": np.ascontiguousarray(inputs[n]) for n in _INS}
    arrays["in_constants"] = constants()
    arrays["in_counts"] = window_counts()
    args = [nc.dram_tensor(n, a.shape, F32, kind="ExternalInput").ap() for n, a in arrays.items()]
    args += [nc.dram_tensor(f"out_{i}", s, F32, kind="ExternalOutput").ap() for i, s in enumerate(_OUTS)]
    args += [[nc.dram_tensor(f"{n}{l}", s, F32, kind="Internal").ap() for l in range(2)]
             for n, s in (("rows", (NTOK, D)), ("results", (2 * NTOK, D)))]
    build(nc, *args)
    r = run_bass_kernel_spmd(nc, [arrays], core_ids=[0])
    return tuple(r.results[0][f"out_{i}"] for i in range(len(_OUTS)))
```
